# Optimizing a Trainium2 kernel written in Bass

```python
import math
import jax
import jax.numpy as jnp
from jax import lax
import numpy as np

D_MODEL = 1024
BATCH = 1
SEQ = 512
DEPTH = 2
DEC_BATCH = 1
DEC_SEQ = 64
PAST_LEN = 512

CHUNK = 64
EPS = 1e-6
D_FF = 2816
PLE_DIM = 256
N_BRANCH = 4
BRANCH_W = 256
CONV_W = 31
CONV_C = 256
HG_HEADS = 4
HG_DK = 64
HG_DV = 64
LIN_BLOCK = 16
HEAD_DIM = 64
SWA_HEADS = 4
SWA_KV_HEADS = 2
SWA_GROUP = SWA_HEADS // SWA_KV_HEADS
WINDOW = 128
WIN_CHUNKS = WINDOW // CHUNK
SB_HEADS = 4
Q_BLOCK = 128

SPLIT_SIZES = (CONV_C, CONV_C,
               HG_HEADS * HG_DK, HG_HEADS * HG_DK, HG_HEADS * HG_DV, HG_HEADS * HG_DV,
               SWA_HEADS * HEAD_DIM, SWA_KV_HEADS * HEAD_DIM, SWA_KV_HEADS * HEAD_DIM,
               SB_HEADS * HEAD_DIM, SB_HEADS * HEAD_DIM, SB_HEADS * HEAD_DIM,
               N_BRANCH * D_MODEL)
D_IN = 2 * CONV_C + 2 * HG_HEADS * HG_DK + 2 * HG_HEADS * HG_DV + (SWA_HEADS + 2 * SWA_KV_HEADS) * HEAD_DIM + 3 * SB_HEADS * HEAD_DIM + N_BRANCH * D_MODEL

kernel_name = "hybrid_streaming_encoder_step"

def _split_points():
    return [int(v) for v in np.cumsum(np.array(SPLIT_SIZES))[:-1]]

def rmsnorm(x, g):
    xf = x.astype(jnp.float32)
    y = xf * lax.rsqrt(jnp.mean(xf * xf, axis=-1, keepdims=True) + EPS)
    return (y * g.astype(jnp.float32)).astype(x.dtype)

def layernorm(x, g, b):
    xf = x.astype(jnp.float32)
    mu = jnp.mean(xf, axis=-1, keepdims=True)
    xc = xf - mu
    y = xc * lax.rsqrt(jnp.mean(xc * xc, axis=-1, keepdims=True) + EPS)
    return (y * g.astype(jnp.float32) + b.astype(jnp.float32)).astype(x.dtype)

def swiglu(x, w_up, w_down):
    a, b = jnp.split(x @ w_up, 2, axis=-1)
    return (jax.nn.silu(a) * b) @ w_down

def alibi_slopes():
    h = jnp.arange(1, SWA_HEADS + 1, dtype=jnp.float32)
    return (2.0 ** (-8.0 * h / SWA_HEADS)).reshape(SWA_KV_HEADS, SWA_GROUP)

def conv_branch(a, b, hist, conv_w, conv_b, ln_g, ln_b):
    z = a * jax.nn.sigmoid(b)
    zc = jnp.concatenate([hist.astype(z.dtype), z], axis=1)
    y = lax.conv_general_dilated(zc, conv_w.astype(z.dtype)[:, None, :], window_strides=(1,), padding='VALID',
                                 dimension_numbers=('NWC', 'WIO', 'NWC'), feature_group_count=CONV_C)
    y = jax.nn.silu(layernorm(y + conv_b, ln_g, ln_b))
    return y, zc[:, -(CONV_W - 1):]

def hgrn_branch(q, fz, i_in, g, s0, lb, norm_g):
    B, L, _ = q.shape
    lbf = lb.astype(jnp.float32)
    fzf = fz.astype(jnp.float32)
    log_f = jnp.log(lbf + (1.0 - lbf) * jax.nn.sigmoid(fzf))
    k = (1.0 - lbf) * jax.nn.sigmoid(-fzf)
    pad = (-L) % LIN_BLOCK
    n = (L + pad) // LIN_BLOCK

    def blocks(t, d):
        t = jnp.pad(t.astype(jnp.float32), ((0, 0), (0, pad), (0, 0)))
        return t.reshape(B, n, LIN_BLOCK, HG_HEADS, d).transpose(1, 0, 3, 2, 4)

    xs = (blocks(q, HG_DK), blocks(k, HG_DK), blocks(log_f, HG_DK), blocks(i_in, HG_DV))
    causal = jnp.tril(jnp.ones((LIN_BLOCK, LIN_BLOCK), dtype=bool))

    def step(S, inp):
        qc, kc, lfc, vc = inp
        G = jnp.cumsum(lfc, axis=2)
        o_inter = jnp.einsum('bhtk,bhkv->bhtv', qc * jnp.exp(G), S)
        decay = jnp.exp(jnp.where(causal[:, :, None], G[:, :, :, None, :] - G[:, :, None, :, :], -jnp.inf))
        attn = jnp.einsum('bhtk,bhtsk,bhsk->bhts', qc, decay, kc)
        o = o_inter + jnp.einsum('bhts,bhsv->bhtv', attn, vc)
        G_last = G[:, :, -1]
        S_new = jnp.exp(G_last)[..., None] * S + jnp.einsum('bhsk,bhsv->bhkv', kc * jnp.exp(G_last[:, :, None] - G), vc)
        return S_new, o

    S_fin, o = lax.scan(step, s0.astype(jnp.float32), xs)
    o = o.transpose(1, 0, 3, 2, 4).reshape(B, n * LIN_BLOCK, HG_HEADS, HG_DV)[:, :L]
    gg = g.astype(jnp.float32).reshape(B, L, HG_HEADS, HG_DV)
    o = rmsnorm(o, norm_g) * jax.nn.silu(gg)
    return o.reshape(B, L, HG_HEADS * HG_DV), S_fin

def sink_attend(s, sinks, v, eq):
    sk = sinks.astype(jnp.float32)[:, :, None, None]
    m = jnp.maximum(jnp.max(s, axis=-1, keepdims=True), sk)
    p = jnp.exp(s - m)
    p = p / (jnp.sum(p, axis=-1, keepdims=True) + jnp.exp(sk - m))
    return jnp.einsum(eq, p.astype(v.dtype), v)

def swa_prompt(q, k, v, sinks):
    B, L = q.shape[:2]
    nC = L // CHUNK
    back = WIN_CHUNKS * CHUNK
    KB = (WIN_CHUNKS + 1) * CHUNK

    def band(t):
        tp = jnp.pad(t, ((0, 0), (back, 0), (0, 0), (0, 0)))
        tp = tp.reshape(B, nC + WIN_CHUNKS, CHUNK, SWA_KV_HEADS, HEAD_DIM)
        return jnp.concatenate([tp[:, j:j + nC] for j in range(WIN_CHUNKS + 1)], axis=2)

    kb, vb = band(k), band(v)
    qc = q.reshape(B, nC, CHUNK, SWA_KV_HEADS, SWA_GROUP, HEAD_DIM)
    c0 = jnp.arange(nC)[:, None] * CHUNK
    q_pos = c0 + jnp.arange(CHUNK)[None]
    k_pos = c0 - back + jnp.arange(KB)[None]
    dist = jnp.abs(q_pos[:, :, None] - k_pos[:, None, :]).astype(jnp.float32)
    s = jnp.einsum('bnqhgd,bnkhd->bnhgqk', qc, kb).astype(jnp.float32) * (HEAD_DIM ** -0.5)
    s = s - alibi_slopes()[:, :, None, None] * dist[None, :, None, None]
    s = jnp.where((k_pos >= 0)[None, :, None, None, None, :], s, -jnp.inf)
    o = sink_attend(s, sinks.reshape(SWA_KV_HEADS, SWA_GROUP), vb, 'bnhgqk,bnkhd->bnqhgd')
    return o.reshape(B, L, SWA_HEADS * HEAD_DIM)

def swa_sample(q, k, v, sinks, k_start):
    B, L = q.shape[:2]
    q_pos = PAST_LEN + jnp.arange(L)
    k_pos = k_start + jnp.arange(k.shape[1])
    dist = jnp.abs(q_pos[:, None] - k_pos[None, :]).astype(jnp.float32)
    s = jnp.einsum('bqhgd,bkhd->bhgqk', q, k).astype(jnp.float32) * (HEAD_DIM ** -0.5)
    s = s - alibi_slopes()[:, :, None, None] * dist
    o = sink_attend(s, sinks.reshape(SWA_KV_HEADS, SWA_GROUP), v, 'bhgqk,bkhd->bqhgd')
    return o.reshape(B, L, SWA_HEADS * HEAD_DIM)

def sb_block(q, k, v, q_pos, k_pos):
    z = jnp.einsum('bqhd,bkhd->bhqk', q, k).astype(jnp.float32) * (HEAD_DIM ** -0.5)
    mask = k_pos[None, :] < q_pos[:, None]
    log_beta = jax.nn.log_sigmoid(z)
    log_1mb = jnp.where(mask, jax.nn.log_sigmoid(-z), 0.0)
    rest = lax.cumsum(log_1mb, axis=3, reverse=True) - log_1mb
    a = jnp.where(mask, jnp.exp(log_beta + rest), 0.0)
    return jnp.einsum('bhqk,bkhd->bqhd', a.astype(v.dtype), v)

def sb_prompt(q, k, v):
    B, L = q.shape[:2]
    nb = L // Q_BLOCK
    qb = q.reshape(B, nb, Q_BLOCK, SB_HEADS, HEAD_DIM).transpose(1, 0, 2, 3, 4)
    k_pos = jnp.arange(L)

    def one(args):
        qi, bi = args
        return sb_block(qi, k, v, bi * Q_BLOCK + jnp.arange(Q_BLOCK), k_pos)

    o = lax.map(one, (qb, jnp.arange(nb)))
    return o.transpose(1, 0, 2, 3, 4).reshape(B, L, SB_HEADS * HEAD_DIM)

def token_mix(u, conv_hist, hg_state, swa_kv, sb_kv, lb, w_in, conv_w, conv_b, cln_g, cln_b,
              hg_norm_g, sinks, w_branch, w_out):
    B, L, _ = u.shape
    ca, cb, hq, hf, hi, hg, sq, sk, sv, bq, bk, bv, gl = jnp.split(u @ w_in, _split_points(), axis=-1)
    o_conv, conv_new = conv_branch(ca, cb, conv_hist, conv_w, conv_b, cln_g, cln_b)
    o_hg, hg_new = hgrn_branch(hq, hf, hi, hg, hg_state, lb, hg_norm_g)
    sq = sq.reshape(B, L, SWA_KV_HEADS, SWA_GROUP, HEAD_DIM)
    sk = sk.reshape(B, L, SWA_KV_HEADS, HEAD_DIM)
    sv = sv.reshape(B, L, SWA_KV_HEADS, HEAD_DIM)
    bq = bq.reshape(B, L, SB_HEADS, HEAD_DIM)
    bk = bk.reshape(B, L, SB_HEADS, HEAD_DIM)
    bv = bv.reshape(B, L, SB_HEADS, HEAD_DIM)
    if swa_kv is None:
        o_swa = swa_prompt(sq, sk, sv, sinks)
        swa_k_all, swa_v_all = sk, sv
    else:
        ck, cv = swa_kv
        swa_k_all = jnp.concatenate([ck.astype(sk.dtype), sk], axis=1)
        swa_v_all = jnp.concatenate([cv.astype(sv.dtype), sv], axis=1)
        o_swa = swa_sample(sq, swa_k_all, swa_v_all, sinks, PAST_LEN - ck.shape[1])
    if sb_kv is None:
        o_sb = sb_prompt(bq, bk, bv)
    else:
        ck, cv = sb_kv
        kk = jnp.concatenate([ck.astype(bk.dtype), bk], axis=1)
        vv = jnp.concatenate([cv.astype(bv.dtype), bv], axis=1)
        o_sb = sb_block(bq, kk, vv, PAST_LEN + jnp.arange(L), jnp.arange(kk.shape[1])).reshape(B, L, SB_HEADS * HEAD_DIM)
    o = jnp.stack([o_conv.astype(u.dtype), o_hg.astype(u.dtype), o_swa.astype(u.dtype), o_sb.astype(u.dtype)], axis=2)
    y = jnp.einsum('blnc,ncd->blnd', o, w_branch)
    gate = jax.nn.sigmoid(gl.reshape(B, L, N_BRANCH, D_MODEL))
    mix = jnp.sum(gate * y, axis=2) @ w_out
    new = (conv_new, hg_new, swa_k_all[:, -WINDOW:], swa_v_all[:, -WINDOW:], bk, bv)
    return mix, new

def trunk_layer(x, pe, conv_hist, hg_state, swa_kv, sb_kv, lb, lw):
    (f1_pre, f1_up, f1_down, f1_post, m_pre, w_in, conv_w, conv_b, cln_g, cln_b, hg_norm_g, sinks,
     w_branch, w_out, m_post, f2_pre, f2_up, f2_down, f2_post, ple_pre, ple_gate_w, ple_w, ple_post) = lw
    h = x + 0.5 * rmsnorm(swiglu(rmsnorm(x, f1_pre), f1_up, f1_down), f1_post)
    mix, new = token_mix(rmsnorm(h, m_pre), conv_hist, hg_state, swa_kv, sb_kv, lb, w_in, conv_w, conv_b,
                         cln_g, cln_b, hg_norm_g, sinks, w_branch, w_out)
    h = h + rmsnorm(mix, m_post)
    h = h + 0.5 * rmsnorm(swiglu(rmsnorm(h, f2_pre), f2_up, f2_down), f2_post)
    e = pe.astype(h.dtype) @ ple_w
    h = h + rmsnorm(e * jax.nn.sigmoid(rmsnorm(h, ple_pre) @ ple_gate_w), ple_post)
    return h, new

def setup_inputs(seed: int = 0) -> dict:
    key = jax.random.key(seed)
    ks = iter(jax.random.split(key, 48))
    f32 = jnp.float32

    def nrm(shape, scale):
        return scale * jax.random.normal(next(ks), shape, f32)

    def gain(shape):
        return 1.0 + 0.05 * jax.random.normal(next(ks), shape, f32)

    Dm = D_MODEL
    return {
        'x_prompt': nrm((BATCH, SEQ, Dm), 1.0),
        'x_sample': nrm((DEC_BATCH, DEC_SEQ, Dm), 1.0),
        'p_prompt': nrm((DEPTH, BATCH, SEQ, PLE_DIM), 1.0),
        'p_sample': nrm((DEPTH, DEC_BATCH, DEC_SEQ, PLE_DIM), 1.0),
        'cache_conv': nrm((DEPTH, DEC_BATCH, CONV_W - 1, CONV_C), 0.5),
        'state_hgrn': nrm((DEPTH, DEC_BATCH, HG_HEADS, HG_DK, HG_DV), 0.5),
        'cache_swa_k': nrm((DEPTH, DEC_BATCH, WINDOW, SWA_KV_HEADS, HEAD_DIM), 1.0),
        'cache_swa_v': nrm((DEPTH, DEC_BATCH, WINDOW, SWA_KV_HEADS, HEAD_DIM), 1.0),
        'cache_sb_k': nrm((DEPTH, DEC_BATCH, PAST_LEN, SB_HEADS, HEAD_DIM), 1.0),
        'cache_sb_v': nrm((DEPTH, DEC_BATCH, PAST_LEN, SB_HEADS, HEAD_DIM), 1.0),
        'ffn1_pre_g': gain((DEPTH, Dm)),
        'ffn1_up': nrm((DEPTH, Dm, 2 * D_FF), Dm ** -0.5),
        'ffn1_down': nrm((DEPTH, D_FF, Dm), D_FF ** -0.5),
        'ffn1_post_g': gain((DEPTH, Dm)),
        'mix_pre_g': gain((DEPTH, Dm)),
        'w_in': nrm((DEPTH, Dm, D_IN), Dm ** -0.5),
        'conv_w': nrm((DEPTH, CONV_W, CONV_C), CONV_W ** -0.5),
        'conv_b': nrm((DEPTH, CONV_C), 0.01),
        'conv_ln_g': gain((DEPTH, CONV_C)),
        'conv_ln_b': nrm((DEPTH, CONV_C), 0.01),
        'hgrn_lb_logits': nrm((DEPTH, HG_HEADS * HG_DK), 1.0),
        'hgrn_norm_g': gain((DEPTH, HG_DV)),
        'swa_sinks': nrm((DEPTH, SWA_HEADS), 0.5),
        'w_branch': nrm((DEPTH, N_BRANCH, BRANCH_W, Dm), BRANCH_W ** -0.5),
        'w_out': nrm((DEPTH, Dm, Dm), Dm ** -0.5),
        'mix_post_g': gain((DEPTH, Dm)),
        'ffn2_pre_g': gain((DEPTH, Dm)),
        'ffn2_up': nrm((DEPTH, Dm, 2 * D_FF), Dm ** -0.5),
        'ffn2_down': nrm((DEPTH, D_FF, Dm), D_FF ** -0.5),
        'ffn2_post_g': gain((DEPTH, Dm)),
        'ple_pre_g': gain((DEPTH, Dm)),
        'ple_gate_w': nrm((DEPTH, Dm, Dm), Dm ** -0.5),
        'ple_w': nrm((DEPTH, PLE_DIM, Dm), PLE_DIM ** -0.5),
        'ple_post_g': gain((DEPTH, Dm)),
    }

def reference(x_prompt, x_sample, p_prompt, p_sample, cache_conv, state_hgrn, cache_swa_k, cache_swa_v,
              cache_sb_k, cache_sb_v, ffn1_pre_g, ffn1_up, ffn1_down, ffn1_post_g, mix_pre_g, w_in, conv_w,
              conv_b, conv_ln_g, conv_ln_b, hgrn_lb_logits, hgrn_norm_g, swa_sinks, w_branch, w_out, mix_post_g,
              ffn2_pre_g, ffn2_up, ffn2_down, ffn2_post_g, ple_pre_g, ple_gate_w, ple_w, ple_post_g):
    lb_soft = jax.nn.softmax(hgrn_lb_logits.astype(jnp.float32), axis=0)
    lb_all = jnp.cumsum(lb_soft, axis=0) - lb_soft[0:1]
    bp = x_prompt.shape[0]
    hp, hs = x_prompt, x_sample
    st_p = [[] for _ in range(6)]
    st_s = [[] for _ in range(6)]
    for i in range(DEPTH):
        lw = (ffn1_pre_g[i], ffn1_up[i], ffn1_down[i], ffn1_post_g[i], mix_pre_g[i], w_in[i], conv_w[i], conv_b[i],
              conv_ln_g[i], conv_ln_b[i], hgrn_norm_g[i], swa_sinks[i], w_branch[i], w_out[i], mix_post_g[i],
              ffn2_pre_g[i], ffn2_up[i], ffn2_down[i], ffn2_post_g[i], ple_pre_g[i], ple_gate_w[i], ple_w[i],
              ple_post_g[i])
        conv0 = jnp.zeros((bp, CONV_W - 1, CONV_C), x_prompt.dtype)
        hg0 = jnp.zeros((bp, HG_HEADS, HG_DK, HG_DV), jnp.float32)
        hp, new_p = trunk_layer(hp, p_prompt[i], conv0, hg0, None, None, lb_all[i], lw)
        hs, new_s = trunk_layer(hs, p_sample[i], cache_conv[i], state_hgrn[i], (cache_swa_k[i], cache_swa_v[i]),
                                (cache_sb_k[i], cache_sb_v[i]), lb_all[i], lw)
        for j in range(6):
            st_p[j].append(new_p[j].astype(x_prompt.dtype))
            st_s[j].append(new_s[j].astype(x_sample.dtype))
    sp = [jnp.stack(a, axis=0) for a in st_p]
    ss = [jnp.stack(a, axis=0) for a in st_s]
    return (hp, hs, sp[0], ss[0], sp[1], ss[1], sp[2], sp[3], ss[2], ss[3], sp[4], sp[5], ss[4], ss[5])


_drawn_inputs = setup_inputs


def setup_inputs(seed=0):
    import zlib

    import numpy as np

    out = dict(_drawn_inputs(seed))
    spreads = {}
    factors = {'conv_b': 5.815,
     'conv_ln_b': 8.0,
     'swa_sinks': 6.415,
     'ffn2_post_g': 3.092,
     'ple_pre_g': 3.922}
    for name, (base, spread) in spreads.items():
        noise = np.random.default_rng([zlib.crc32(name.encode()), seed]).standard_normal(out[name].shape)
        drawn = base * np.exp(spread * noise) if base else spread * noise
        out[name] = jnp.asarray(drawn.astype(out[name].dtype))
    for name, factor in factors.items():
        out[name] = (out[name] * factor).astype(out[name].dtype)
    return out
```

```python
from contextlib import ExitStack

import concourse.bass as bass
from concourse import mybir

F32 = mybir.dt.float32
F32R = mybir.dt.float32r
ALU = mybir.AluOpType
ACT = mybir.ActivationFunctionType
AX = mybir.AxisListType

D = 1024
SEQ, DEC = 512, 64
T = SEQ + DEC
HT = T // 2
DEPTH = 2
PAST = 512
CHUNK = 64
EPS = 1e-6
FF = 2816
PLE = 256
NB = 4
CW = 31
HIST = CW - 1
WINDOW = 128
HD = 64
KD = D // 128
KF = FF // 128
LB = 16
NBLK = T // LB
NBLK_P = SEQ // LB
TB = (T + 127) // 128
SLOPES = [2.0 ** (-8.0 * (h + 1) / 4) for h in range(4)]

C_CA, C_CB, C_HQ, C_HF, C_HI, C_HG = 0, 256, 512, 768, 1024, 1280
C_SQ, C_SK, C_SV, C_BQ, C_BK, C_BV, C_GATE = 1536, 1792, 1920, 2048, 2304, 2560, 2816
F_, Q_, V_, G_, CA_, CB_, SQ_, SK_, SV_, BQ_, BK_, BV_ = 0, 2, 4, 6, 8, 10, 12, 14, 15, 16, 18, 20
NPROJ = 22
PROJ_COL = {F_: C_HF, Q_: C_HQ, V_: C_HI, G_: C_HG, CA_: C_CA, CB_: C_CB, BQ_: C_BQ, BK_: C_BK, BV_: C_BV}

U_UP, U_DOWN = 2 * KF, 3 * KD
U_FFN = U_UP + U_DOWN
U_MIX = NPROJ + 5 * KD + KD
U0_FFN1 = 0
U0_PROJ = U_FFN
U0_GATE = U0_PROJ + NPROJ
U0_PAIR = U0_GATE + 2 * KD
U0_OUT = U0_GATE + 5 * KD
U0_FFN2 = U0_OUT + KD
U0_PLEW = U0_FFN2 + U_FFN
U0_PLEG = U0_PLEW + 2
UNITS = U0_PLEG + KD
RAW = 4
SPLIT = 2
DOWN_K = [(0, 8), (8, 16), (16, KF)]

N_F1PRE, N_F1POST, N_MPRE, N_MPOST, N_F2PRE, N_F2POST, N_PPRE, N_PPOST = range(8)
R_CONVW, R_CONVB, R_LNG, R_LNB, R_HGN = 0, 62, 64, 66, 68
NROW2 = 69


def trunk(nc, a, o):
    n_consts = [0]
    n_placed = [0]
    with ExitStack() as ctx:
        base = nc.sbuf_base
        arena = ctx.enter_context(nc.sbuf_tensor("arena", [128, (nc.sbuf_usable_end - base) // 4 - 16], F32))
        limit = nc.sbuf_usable_end

        class Region:

            def __init__(self, at):
                self.at = at

            def __call__(self, name, shape, dt=F32, parts=128):
                n = 4
                for s in shape:
                    n *= s
                at = (self.at + 31) // 32 * 32
                self.at = at + n
                assert self.at <= limit, (name, self.at, limit)
                return nc.alloc_sbuf_tensor_at(name, [parts, *shape], dt, offset=at)

        def sem(name):
            return ctx.enter_context(nc.semaphore(name))

        keep = Region((base + 31) // 32 * 32)
        h = keep("h", [KD, T])
        wraw = keep("wraw", [RAW, 1024])
        whi = keep("whi", [SPLIT, 1024], F32R)
        wlo = keep("wlo", [SPLIT, 1024], F32R)
        ident = keep("ident", [128])
        ones = keep("ones", [128])
        headones = keep("headones", [128])
        trineg = keep("trineg", [128])
        negones = keep("negones", [128])
        later = keep("later", [128])
        blockmask = keep("blockmask", [8])
        alibi = keep("alibi", [2, WINDOW + CHUNK])
        blockend = keep("blockend", [T])
        eps_col = keep("eps_col", [1])
        gains = keep("gains", [64])
        par = keep("par", [NROW2])
        lb_all = keep("lb_all", [DEPTH, 2])
        lb = keep("lb", [2])
        lb1m = keep("lb1m", [2])
        sink4 = keep("sink4", [4])
        sinkcol = keep("sinkcol", [2])
        sq = keep("sq", [2, T])
        sqsum = keep("sqsum", [T])
        std = keep("std", [T])
        rstd = keep("rstd", [T])

        u_at = keep.at
        ru = Region(u_at)
        u_hi = ru("u_hi", [KD, T], F32R)
        u_lo = ru("u_lo", [KD, T], F32R)
        y = Region(u_at)("y", [KD, T])
        rf = Region(ru.at)
        s_hi = rf("s_hi", [KF, T], F32R)
        s_lo = rf("s_lo", [KF, T], F32R)
        uf = Region(ru.at)("uf", [2, T])
        silu_a = sq

        rm = Region(ru.at)
        rcache = Region(ru.at)
        chist = rcache("chist", [256])
        ctail = rcache("ctail", [4, 128])
        swk_c = rcache("swk_c", [128])
        swv_c = rcache("swv_c", [2, 128])
        rm("muf", [2, T])
        proj_at = rm.at
        proj = rm("proj", [NPROJ, T])
        of = rm("of", [2 * NB, T])
        tmp_at = rm.at
        rh = Region(tmp_at)
        kgate = rh("kgate", [2, T])
        gpre = rh("gpre", [2, T])
        dsuf = rh("dsuf", [2, T])
        kvtok = rh("kvtok", [2, 512])
        vmask = [rh("vmask", [2, 8, HD]), sq[:].rearrange("p a n -> p (a n)")[:, 0:16 * HD].rearrange("p (a b v) -> p a b v", a=2, b=8)]
        states = rh("states", [2, 2, 9, HD])
        hgs0 = rh("hgs0", [2, HD])
        glast = sqsum[:, 0:2 * NBLK].rearrange("p (c b) -> p c b", c=2)
        rc = Region(tmp_at)
        ZW = HIST + SEQ + HIST + DEC
        YW = ZW - HIST
        zc = rc("zc", [2, ZW])
        yc = rc("yc", [2, YW])
        xc = rc("xc", [2, T])
        rs = Region(tmp_at)
        swkT_c = rs("swkT_c", [128])
        v64 = rs("v64", [11, 128])
        swk_tok = rs("swk_tok", [2, 128])
        sc = rs("sc", [2, 2, 192])
        pT = rs("pT", [2, 2, 3, 128])
        stat = rs("stat", [2, 6, 2])
        rbc = Region(limit - 8192 - 32)
        sbk_c = rbc("sbk_c", [4, 256])
        sbv_c = rbc("sbv_c", [4, 256])
        assert rs.at <= limit - 8224
        rb = Region(tmp_at)
        sbkT_c = rb("sbkT_c", [2, SEQ])
        sbtok = rb("sbtok", [TB, 512])
        spx = rb("spx", [2, 512])
        arg = rb("arg", [2, 512])
        gkeep = proj
        m_split = Region(proj_at)("m_split", [KD, 2, T], F32R)
        ro = Region(proj_at + 16 * T * 4)
        ybr = ro("ybr", [NB, T])
        sg = ro("sg", [2, T])
        assert ro.at <= proj_at + NPROJ * T * 4
        o_lo = Region(proj_at + NPROJ * T * 4)("o_lo", [2 * NB, T], F32R)
        rq = Region(tmp_at)
        o_hi = rq("o_hi", [2 * NB, T], F32R)
        mprod = rq("mprod", [2, T])
        msum = rq("msum", [T])
        rp = Region(ru.at)
        puf = rp("puf", [2, T])
        ptok = rp("ptok", [TB, PLE])
        p_hi = rp("p_hi", [2, T], F32R)
        p_lo = rp("p_lo", [2, T], F32R)
        pf = rp("pf", [2, T])
        e = rp("e", [KD, T])
        gsig = rp("gsig", [2, T])
        rr = Region(ru.at)
        prow = rr("prow", [2, 128])
        prow_end = rr.at
        xtok = Region(prow_end)("xtok", [TB, D])

        ps = ctx.enter_context(nc.psum_tensor("ps", [128, 8, 512], F32))

        def pair(p):
            return ps[:, 2 * p:2 * p + 2, 0:HT]

        def flat(p):
            return ps[:, 2 * p:2 * p + 2, :].rearrange("p a n -> p (a n)")[:, 0:T]

        def halves(ap):
            return ap.rearrange("p (a n) -> p a n", a=2)

        consts_done = sem("consts_done")
        tok_loaded = sem("tok_loaded")
        turned = sem("turned")
        placed = sem("placed")
        out_tok = sem("out_tok")
        w_loaded = [sem(f"w_loaded{i}") for i in range(RAW)]
        w_rounded = sem("w_rounded")
        w_split = sem("w_split")
        unit_done = sem("unit_done")
        par_loaded = sem("par_loaded")
        par_turned = sem("par_turned")
        par_ready = sem("par_ready")
        sq_ready = sem("sq_ready")
        sq_added = sem("sq_added")
        norm_sum = sem("norm_sum")
        std_ready = sem("std_ready")
        h_ready = sem("h_ready")
        u_full = sem("u_full")
        u_high = sem("u_high")
        u_ready = sem("u_ready")
        silu_done = sem("silu_done")
        up_mul = sem("up_mul")
        s_high = sem("s_high")
        s_ready = sem("s_ready")
        y_ready = sem("y_ready")
        dve_step = sem("dve_step")
        act_step = sem("act_step")
        proj_out = sem("proj_out")
        cache_in = sem("cache_in")
        outs = sem("outs")
        hg_kd = sem("hg_kd")
        hg_turned = sem("hg_turned")
        hg_tok = sem("hg_tok")
        hg_vm = sem("hg_vm")
        hg_upd = sem("hg_upd")
        hg_state = sem("hg_state")
        hg_inter = sem("hg_inter")
        hg_inter_in = sem("hg_inter_in")
        hg_w = sem("hg_w")
        hg_att = sem("hg_att")
        hg_acc = sem("hg_acc")
        hg_o = sem("hg_o")
        hg_done = sem("hg_done")
        gate_out = sem("gate_out")
        hg_sq = sem("hg_sq")
        hg_ss = sem("hg_ss")
        hg_std = sem("hg_std")
        cv_hist = sem("cv_hist")
        cv_z = sem("cv_z")
        cv_y = sem("cv_y")
        cv_mean = sem("cv_mean")
        cv_xc = sem("cv_xc")
        cv_sq = sem("cv_sq")
        cv_var = sem("cv_var")
        cv_std = sem("cv_std")
        cv_norm = sem("cv_norm")
        cv_tail = sem("cv_tail")
        cv_out = sem("cv_out")
        sw_turn = sem("sw_turn")
        sw_tok = sem("sw_tok")
        sw_score = sem("sw_score")
        sw_scaled = sem("sw_scaled")
        sw_max = sem("sw_max")
        sw_exp = sem("sw_exp")
        sw_prob = sem("sw_prob")
        sw_pT = sem("sw_pT")
        sw_pTs = sem("sw_pTs")
        sw_pv = sem("sw_pv")
        sw_o = sem("sw_o")
        sb_turn = sem("sb_turn")
        sb_tok = sem("sb_tok")
        sb_z = sem("sb_z")
        sb_zrow = sem("sb_zrow")
        sb_ln = sem("sb_ln")
        sb_sp = sem("sb_sp")
        sb_arg = sem("sb_arg")
        sb_sum = sem("sb_sum")
        sb_min = sem("sb_min")
        sb_exp = sem("sb_exp")
        sb_a = sem("sb_a")
        sb_pv = sem("sb_pv")
        sb_o = sem("sb_o")
        o_high = sem("o_high")
        o_ready = sem("o_ready")
        yb_out = sem("yb_out")
        sig_done = sem("sig_done")
        gated = sem("gated")
        m_ready = sem("m_ready")
        p_turned = sem("p_turned")
        p_full = sem("p_full")
        p_high = sem("p_high")
        p_ready = sem("p_ready")
        tok_ple = sem("tok_ple")
        ple_sig = sem("ple_sig")
        e_gated = sem("e_gated")
        e_out = sem("e_out")
        per_layer = [x for x in locals().values() if isinstance(x, bass.SemaphoreHandle)]
        per_layer = [x for x in per_layer if x not in (consts_done, tok_loaded, turned, placed, out_tok)] + w_loaded

        with nc.Block() as block:
            NT = SEQ // 128

            @block.sync
            def _(sp_):
                sp_.dma_start(xtok[:, 0:NT, :], a["x_prompt"][0].rearrange("(t p) d -> p t d", p=128)).then_inc(tok_loaded, 16)
                sp_.dma_start(xtok[0:DEC, NT, :], a["x_sample"][0]).then_inc(tok_loaded, 16)
                sp_.dma_start(prow[0:2 * DEPTH, 0, :], a["hgrn_lb_logits"].rearrange("l (c p) -> (l c) p", p=128)).then_inc(tok_loaded, 16)

            @block.gpsimd
            def _(pool):
                n = [0]

                def link(ins):
                    n[0] += 1
                    ins.then_inc(consts_done, 1)
                    pool.wait_ge(consts_done, n[0])

                link(pool.memset(ident[:], 0.0))
                link(pool.affine_select(out=ident[:], in_=ident[:], compare_op=ALU.not_equal, fill=1.0, base=0,
                                        pattern=[[-1, 128]], channel_multiplier=1))
                link(pool.memset(ones[:], 1.0))
                link(pool.memset(negones[:], -1.0))
                link(pool.memset(eps_col[:], EPS))
                link(pool.memset(headones[:], 0.0))
                link(pool.memset(headones[0:64, 0:64], 1.0))
                link(pool.memset(headones[64:128, 64:128], 1.0))
                link(pool.affine_select(out=trineg[:], in_=negones[:], compare_op=ALU.is_ge, fill=0.0, base=0,
                                        pattern=[[-1, 128]], channel_multiplier=1))
                link(pool.affine_select(out=later[:], in_=ones[:], compare_op=ALU.is_gt, fill=0.0, base=0,
                                        pattern=[[1, 128]], channel_multiplier=-1))
                link(pool.affine_select(out=blockmask[:], in_=ones[:, 0:8], compare_op=ALU.is_ge, fill=0.0, base=0,
                                        pattern=[[-LB, 8]], channel_multiplier=1))
                link(pool.affine_select(out=blockmask[:], in_=blockmask[:], compare_op=ALU.is_ge, fill=0.0, base=LB - 1,
                                        pattern=[[LB, 8]], channel_multiplier=-1))
                link(pool.memset(blockend[:], 0.0))
                link(pool.memset(blockend[:].rearrange("p (b t) -> p b t", t=LB)[:, :, LB - 1:LB], 1.0))
                for g in range(2):
                    half = slice(64 * g, 64 * g + 64)
                    for v in range(2):
                        link(pool.iota(alibi[half, v, :], pattern=[[-1, WINDOW + CHUNK]], base=WINDOW, channel_multiplier=1,
                                       allow_small_or_imprecise_dtypes=True))
                        neg = wraw[half, v, 0:WINDOW + CHUNK]
                        link(pool.tensor_scalar(neg, alibi[half, v, :], 0.0, SLOPES[2 * v + g], ALU.min, ALU.mult))
                        link(pool.tensor_scalar(alibi[half, v, :], alibi[half, v, :], 0.0, -SLOPES[2 * v + g], ALU.max, ALU.mult))
                        link(pool.tensor_tensor(alibi[half, v, :], alibi[half, v, :], neg, ALU.add))
                n_consts[0] = n[0]

            @block.tensor
            def _(pe):
                pe.wait_ge(consts_done, n_consts[0])
                pe.wait_ge(tok_loaded, 48)
                for k in range(KD):
                    if k >= 4:
                        pe.wait_ge(placed, k - 3)
                    for t in range(TB):
                        n = min(128, T - 128 * t)
                        ins = pe.transpose(flat(k % 4)[:, 128 * t:128 * t + n], xtok[0:n, t, 128 * k:128 * k + 128], ident[0:n, 0:n])
                    ins.then_inc(turned, 1)
                pe.wait_ge(placed, KD)
                pe.transpose(ps[:, 0, 0:2 * DEPTH], prow[0:2 * DEPTH, 0, :], ident[0:2 * DEPTH, 0:2 * DEPTH]).then_inc(turned, 1)

            @block.vector
            def _(dve):
                for k in range(KD):
                    dve.wait_ge(turned, k + 1)
                    dve.tensor_copy(h[:, k, :], flat(k % 4)).then_inc(placed, 1)
                dve.wait_ge(turned, KD + 1)
                n = [KD]

                def link(ins):
                    n[0] += 1
                    ins.then_inc(placed, 1)
                    dve.wait_ge(placed, n[0])

                lg, mx, sm = std[:, 0:4], std[:, 4:6], std[:, 6:8]
                link(dve.tensor_copy(lg, ps[:, 0, 0:4]))
                link(dve.tensor_tensor(mx, lg[:, 0:2], lg[:, 2:4], ALU.max))
                link(dve.tensor_tensor(lg[:, 0:2], lg[:, 0:2], mx, ALU.subtract))
                link(dve.tensor_tensor(lg[:, 2:4], lg[:, 2:4], mx, ALU.subtract))
                dve.wait_ge(turned, KD + 2)
                link(dve.tensor_tensor(sm, lg[:, 0:2], lg[:, 2:4], ALU.add))
                link(dve.reciprocal(sm, sm))
                link(dve.tensor_tensor(lg[:, 0:2], lg[:, 0:2], sm, ALU.mult))
                link(dve.tensor_tensor(lg[:, 2:4], lg[:, 2:4], sm, ALU.mult))
                link(dve.tensor_tensor(lb_all[:, 0, :], lg[:, 0:2], lg[:, 0:2], ALU.subtract))
                link(dve.tensor_tensor(lb_all[:, 1, :], lg[:, 0:2], lg[:, 2:4], ALU.add))
                link(dve.tensor_tensor(lb_all[:, 1, :], lb_all[:, 1, :], lg[:, 0:2], ALU.subtract))
                n_placed[0] = n[0]

            @block.scalar
            def _(act):
                act.wait_ge(placed, KD + 4)
                act.activation(std[:, 0:4], std[:, 0:4], ACT.Exp).then_inc(turned, 1)


        def done(i):
            return i + 1 + SPLIT

        def load_unit(sp_, slot, i, src, n=8):
            sp_.wait_ge(w_split, i + 1)
            sp_.dma_start(wraw[:, slot, 0:128 * n].rearrange("p (k n) -> p k n", k=n), src).then_inc(w_loaded[slot], 16)

        def cols(w, L, c, k0=0, nk=8):
            v = w[bass.ds(L, 1), 128 * k0:128 * (k0 + nk), c].rearrange("l (k p) n -> p (l k) n", p=128)
            return v

        def load_ffn(sp_, L, up, down, u0):
            with sp_.Fori(0, KF // 2) as it:
                for q in range(4):
                    c = bass.ds(it * 256 + 128 * (q // 2) + FF * (q % 2), 128)
                    load_unit(sp_, (u0 + q) % RAW, it * 4 + (u0 + q), cols(up, L, c))
            with sp_.Fori(0, 2) as it:
                for m in range(4):
                    for q, (k0, k1) in enumerate(DOWN_K):
                        i = U_UP + 3 * m + q
                        load_unit(sp_, (u0 + i) % RAW, it * 12 + (u0 + i), cols(down, L, bass.ds(it * 512 + 128 * m, 128), k0, k1 - k0), k1 - k0)

        def products(pe, part, x_hi, x_lo, ks, k_off, p, start, stop, wait_k=None):
            ins = None
            for n, k in enumerate(ks):
                if wait_k is not None:
                    wait_k(k)
                w = slice(128 * (k_off + n), 128 * (k_off + n) + 128)
                for c, (wt, x) in enumerate(((whi, x_hi), (whi, x_lo), (wlo, x_hi))):
                    for f in range(2):
                        ins = pe.matmul(ps[:, 2 * p + f, 0:HT], wt[:, part, w], x[:, k, HT * f:HT * f + HT],
                                        start=start and n == 0 and c == 0, stop=stop and n == len(ks) - 1 and c == 2,
                                        skip_group_check=True)
            return ins

        def split_ready(pe, i):
            pe.wait_ge(w_split, i + 1 + RAW)

        def ones_product(pe, p, w, x, start=True, stop=True):
            for f in range(2):
                ins = pe.matmul(ps[:, 2 * p + f, 0:HT], w, x[:, HT * f:HT * f + HT], start=start, stop=stop)
            return ins

        def pe_norm(pe, n, p):
            pe.wait_ge(sq_added, 8 * n + 8)
            ones_product(pe, p, ones[:], sqsum).then_inc(norm_sum, 1)

        def pe_ffn(pe, f, u0):
            pe_norm(pe, 4 * f + N_F1PRE, 0)
            pn = 2 * f
            with pe.Fori(0, KF // 2) as it:
                for q in range(4):
                    i = it * 4 + (u0 + q)
                    split_ready(pe, i)
                    if q == 0:
                        pe.wait_ge(u_ready, 8 * pn + 8)
                    pe.wait_ge(up_mul, it * 2 + (f * KF + q // 2 + 1))
                    products(pe, (u0 + q) % SPLIT, u_hi, u_lo, range(KD), 0, q, True, True).then_inc(unit_done, 1)
            with pe.Fori(0, 2) as it:
                for m in range(4):
                    for q, (k0, k1) in enumerate(DOWN_K):
                        i = it * 12 + (u0 + U_UP + 3 * m + q)
                        split_ready(pe, i)
                        if q == 0:
                            pe.wait_ge(y_ready, it * 4 + (m + 1 + y_before[4 * f + N_F1POST]))
                        if m == 0 and q != 1:
                            pe.wait_ge(s_ready, f * KF + 2 + (KF - 1 if q == 0 else KF))
                        products(pe, (u0 + U_UP + 3 * m + q) % SPLIT, s_hi, s_lo, range(k0, k1), 0, m, q == 0, q == 2).then_inc(unit_done, 1)
            pe_norm(pe, 4 * f + N_F1POST, 0)

        y_before = {N_F1POST: 0, N_MPOST: 8, N_F2POST: 16, N_PPOST: 24}

        def act_square(act, n, k, src):
            if 8 * n + k >= 2:
                act.wait_ge(sq_added, 8 * n + k - 1)
            act.activation(sq[:, k % 2, :] if src.ndim == 2 else halves(sq[:, k % 2, :]), src, ACT.Square).then_inc(sq_ready, 1)

        def act_norm_h(act, n):
            pn = n // 2
            for k in range(KD):
                if pn:
                    act.wait_ge(h_ready, 8 * (pn - 1) + k + 1)
                act_square(act, n, k, h[:, k, :])
            act_root(act, n, 0)
            for k in range(KD):
                act.wait_ge(u_full, 8 * pn + k + 1)
                act.activation(u_hi[:, k, :], uf[:, k % 2, :], ACT.Copy).then_inc(u_high, 1)

        def act_root(act, n, p):
            act.wait_ge(norm_sum, n + 1)
            act.activation(halves(std[:]), pair(p), ACT.Sqrt, bias=eps_col[:], scale=1.0 / D).then_inc(std_ready, 1)

        def act_y(act, n, m, unit, p):
            act.wait_ge(unit_done, done(unit))
            act_square(act, n, m, pair(p))
            act.activation(halves(y[:, m, :]), pair(p), ACT.Copy).then_inc(y_ready, 1)

        def act_ffn(act, f, u0):
            act_norm_h(act, 4 * f + N_F1PRE)
            with act.Fori(0, KF // 2) as it:
                for q in range(2):
                    act.wait_ge(unit_done, it * 4 + done(u0 + 2 * q))
                    act.wait_ge(s_ready, it * 2 + (f * KF + q + 1))
                    act.activation(halves(silu_a[:, q, :]), pair(2 * q), ACT.Silu).then_inc(silu_done, 1)
            for m in range(KD):
                act_y(act, 4 * f + N_F1POST, m, u0 + U_UP + 3 * m + 2, m % 4)
            act_root(act, 4 * f + N_F1POST, 0)

        steps = [0]

        def link(dve, ins):
            steps[0] += 1
            ins.then_inc(dve_step, 1)
            dve.wait_ge(dve_step, steps[0])

        def dve_add_square(dve, n, k):
            dve.wait_ge(sq_ready, 8 * n + k + 1)
            if k == 0:
                if n:
                    dve.wait_ge(norm_sum, n)
                dve.tensor_copy(sqsum[:], sq[:, 0, :]).then_inc(sq_added, 1)
            else:
                dve.wait_ge(sq_added, 8 * n + k)
                dve.tensor_tensor(sqsum[:], sqsum[:], sq[:, k % 2, :], ALU.add).then_inc(sq_added, 1)

        def dve_rstd(dve, n):
            dve.wait_ge(std_ready, n + 1)
            link(dve, dve.reciprocal(rstd[:], std[:]))

        def dve_apply(dve, n):
            pn = n // 2

            def low(k):
                dve.wait_ge(u_high, 8 * pn + k + 1)
                dve.tensor_tensor(u_lo[:, k, :], uf[:, k % 2, :], u_hi[:, k, :], ALU.subtract).then_inc(u_ready, 1)

            dve_rstd(dve, n)
            for k in range(KD):
                if k >= 2:
                    dve.wait_ge(u_ready, 8 * pn + k - 1)
                dve.scalar_tensor_tensor(out=uf[:, k % 2, :], in0=h[:, k, :], scalar=gains[:, 8 * n + k:8 * n + k + 1],
                                         in1=rstd[:], op0=ALU.mult, op1=ALU.mult).then_inc(u_full, 1)
                if k:
                    low(k - 1)
            low(KD - 1)

        def dve_residual(dve, n, src):
            pn = n // 2
            dve_rstd(dve, n)
            for k in range(KD):
                if n != N_PPOST:
                    dve.wait_ge(y_ready, 4 + y_before[n] + k + 1)
                link(dve, dve.scalar_tensor_tensor(out=uf[:, k % 2, :], in0=src[:, k, :], scalar=gains[:, 8 * n + k:8 * n + k + 1],
                                                   in1=rstd[:], op0=ALU.mult, op1=ALU.mult))
                dve.tensor_tensor(h[:, k, :], h[:, k, :], uf[:, k % 2, :], ALU.add).then_inc(h_ready, 1)
                if n < 7 and k:
                    dve_add_square(dve, n + 1, k - 1)
            if n < 7:
                dve_add_square(dve, n + 1, KD - 1)

        def dve_ffn(dve, f, u0):
            dve_apply(dve, 4 * f + N_F1PRE)
            with dve.Fori(0, KF // 2) as it:
                for q in range(2):
                    x = silu_a[:, q, :]
                    dve.wait_ge(unit_done, it * 4 + done(u0 + 2 * q + 1))
                    dve.wait_ge(silu_done, it * 2 + (f * KF + q + 1))
                    dve.tensor_tensor(halves(x), halves(x), pair(2 * q + 1), ALU.mult).then_inc(up_mul, 1)
                    dve.wait_ge(up_mul, it * 2 + (f * KF + q + 1 + 2))
                    dve.tensor_scalar(s_hi[:, bass.ds(it * 2 + q, 1), :].rearrange("p a n -> p (a n)"), x, 1.0, None, ALU.mult).then_inc(s_high, 1)
                    dve.wait_ge(s_high, it * 2 + (f * KF + q + 1))
                    dve.tensor_tensor(s_lo[:, bass.ds(it * 2 + q, 1), :].rearrange("p a n -> p (a n)"), x,
                                      s_hi[:, bass.ds(it * 2 + q, 1), :].rearrange("p a n -> p (a n)"), ALU.subtract).then_inc(s_ready, 1)
            for m in range(KD):
                dve_add_square(dve, 4 * f + N_F1POST, m)

        layer = [None]
        N_OUTS = 14
        CACHE_HG, CACHE_SHORT, CACHE_SB = 4 * 16, 4 * 16, 6 * 16
        asteps = [0]

        def act_link(act, ins):
            asteps[0] += 1
            ins.then_inc(act_step, 1)
            act.wait_ge(act_step, asteps[0])

        def pe_proj(pe, t):
            i = U0_PROJ + t
            split_ready(pe, i)
            if t == 0:
                pe.wait_ge(u_ready, 16)
            if t >= 2:
                pe.wait_ge(proj_out, t - 1)
            products(pe, i % SPLIT, u_hi, u_lo, range(KD), 0, t % 2, True, True).then_inc(unit_done, 1)

        next_proj = [0]
        q_sw = proj[:, SQ_:SQ_ + 2, :].rearrange("p a n -> p (a n)").rearrange("p (c g t) -> p c g t", g=2, t=CHUNK)

        def act_proj_some(act, n):
            for t in range(next_proj[0], next_proj[0] + n):
                act.wait_ge(unit_done, done(U0_PROJ + t))
                x, y_ = halves(proj[:, t, :]), pair(t % 2)
                if t in (F_, F_ + 1):
                    act.activation(halves(kgate[:, t, :]), y_, ACT.Sigmoid, scale=-1.0)
                    ins = act.activation(x, y_, ACT.Sigmoid)
                elif t in (G_, G_ + 1):
                    ins = act.activation(x, y_, ACT.Silu)
                elif t in (CB_, CB_ + 1):
                    ins = act.activation(x, y_, ACT.Sigmoid)
                elif t in (SQ_, SQ_ + 1):
                    for c0, c1, r0, r1 in ((0, 4, 0, 64), (4, 5, 0, 32), (4, 5, 32, 64), (5, 9, 0, 64)):
                        t0 = CHUNK * c0 + r0
                        src = ps[:, 2 * (t % 2) + t0 // HT, t0 % HT:t0 % HT + (c1 - c0) * (r1 - r0)]
                        ins = act.activation(q_sw[:, c0:c1, t - SQ_, r0:r1], src.rearrange("p (c t) -> p c t", c=c1 - c0), ACT.Copy)
                else:
                    ins = act.activation(x, y_, ACT.Copy, scale=HD ** -0.5 if t in (BQ_, BQ_ + 1) else 1.0)
                ins.then_inc(proj_out, 1)
            next_proj[0] += n

        def tok_n(tb):
            return min(128, T - 128 * tb)

        def nblk(tb):
            return tok_n(tb) // LB

        def hg_turn(pe, tb):
            if tb == 0:
                pe.wait_ge(hg_kd, 2)
                pe.wait_ge(proj_out, V_ + 2)
            if tb >= 1:
                pe.wait_ge(hg_tok, tb)
            n, t0 = tok_n(tb), 128 * tb
            for q, x in enumerate((dsuf[:, 0, :], dsuf[:, 1, :], proj[:, V_, :], proj[:, V_ + 1, :])):
                ins = pe.transpose(ps[0:n, 4, 128 * q:128 * q + 128], x[:, t0:t0 + n], ident[:])
            ins.then_inc(hg_turned, 1)

        def hg_update(pe, tb, c):
            n = tok_n(tb)
            pe.wait_ge(hg_vm, 2 * tb + c + 1)
            if tb:
                pe.wait_ge(hg_state, tb)
            for a2 in range(2):
                ins = pe.matmul(ps[64 * a2:64 * a2 + 64, 6 + c, 0:HD * nblk(tb)], kvtok[0:n, tb % 2, 64 * (2 * c + a2):64 * (2 * c + a2) + 64],
                                vmask[c][0:n, a2, 0:nblk(tb), :].rearrange("p b v -> p (b v)"), start=True, stop=True)
            ins.then_inc(hg_upd, 1)

        def hg_states_out(pe, tb):
            pe.wait_ge(hg_state, tb + 1)
            if tb:
                pe.wait_ge(hg_inter_in, tb)
            for b in range(nblk(tb)):
                for c in range(2):
                    for a2 in range(2):
                        hh = slice(64 * a2, 64 * a2 + 64)
                        t0 = 128 * tb + LB * b
                        ins = pe.matmul(ps[hh, 5, 128 * c + LB * b:128 * c + LB * b + LB], states[hh, tb % 2, c, b, :],
                                        gpre[hh, c, t0:t0 + LB], start=True, stop=True)
            ins.then_inc(hg_inter, 1)

        def blocks(ap):
            return ap.rearrange("p (b t) -> p b t", t=LB)

        def hg_distance(pe, s_):
            d, c = divmod(s_, 2)
            n = NBLK // 2 * (LB - d)
            pe.wait_ge(hg_w, s_ + 1)
            if s_ >= 2:
                pe.wait_ge(hg_acc, s_ - 1)
            if s_ < 2:
                pe.wait_ge(hg_inter_in, TB)
            for f in range(2):
                ins = pe.matmul(ps[:, 4 + 2 * c + f, 0:n], headones[:], sq[:, c, n * f:n * f + n], start=True, stop=True)
            ins.then_inc(hg_att, 1)

        def hg_norm_pe(pe, c):
            pe.wait_ge(hg_sq, c + 1)
            ones_product(pe, 2 + c, headones[:], sq[:, c, :]).then_inc(hg_ss, 1)

        def act_hg(act):
            for tb in range(TB):
                n = tok_n(tb)
                act.wait_ge(hg_turned, tb + 1)
                if tb >= 2:
                    act.wait_ge(hg_upd, 2 * (tb - 1))
                    act.wait_ge(hg_vm, 2 * (tb - 1))
                act.activation(kvtok[0:n, tb % 2, :], ps[0:n, 4, :], ACT.Copy).then_inc(hg_tok, 1)
                act_proj_some(act, 1)

        def act_hg_out(act, L):
            act.wait_ge(hg_state, TB)
            for name, tile, last in (("hgrn_prompt", TB - 2, 8), ("hgrn_sample", TB - 1, 4)):
                act.dma_start(o[name][bass.ds(L, 1), 0].rearrange("l (c a) k v -> (a k) (l c) v", a=2), states[:, tile % 2, :, last, :]).then_inc(outs, 16)

        def act_hg_norm(act):
            for c in range(2):
                act.wait_ge(hg_o, c + 1)
                act.activation(sq[:, c, :], of[:, 2 + c, :], ACT.Square).then_inc(hg_sq, 1)
            for c in range(2):
                act.wait_ge(hg_ss, c + 1)
                act.activation(halves((std, sqsum)[c][:]), pair(2 + c), ACT.Sqrt, bias=eps_col[:], scale=1.0 / HD).then_inc(hg_std, 1)

        def dve_hg(dve):
            lk = lambda ins: link(dve, ins)
            dve.wait_ge(par_ready, 8)
            lk(dve.tensor_copy(lb[:], lb_all[:, bass.ds(layer[0], 1), :].rearrange("p a c -> p (a c)")))
            lk(dve.tensor_scalar(lb1m[:], lb[:], -1.0, 1.0, ALU.mult, ALU.add))
            for c in range(2):
                f, k = proj[:, F_ + c, :], kgate[:, c, :]
                dve.wait_ge(proj_out, F_ + c + 1)
                lk(dve.tensor_scalar(f, f, lb1m[:, c:c + 1], lb[:, c:c + 1], ALU.mult, ALU.add))
                lk(dve.tensor_scalar(k, k, lb1m[:, c:c + 1], None, ALU.mult))
                lk(dve.memset(dsuf[:, c, :], 0.0))
                lk(dve.tensor_copy(blocks(dsuf[:, c, :])[:, :, 0:1], blocks(f)[:, :, 0:1]))
                lk(dve.memset(blocks(f)[:, :, 0:1], 0.0))
                lk(dve.tensor_tensor_scan(gpre[:, c, :], f, dsuf[:, c, :], 0.0, ALU.mult, ALU.add))
                lk(dve.memset(dsuf[:, c, T - 1:T], 1.0))
                lk(dve.tensor_tensor_scan(dsuf[:, c, 0:T - 1][:, ::-1], f[:, 1:T][:, ::-1], blockend[:, 0:T - 1][:, ::-1],
                                          1.0, ALU.mult, ALU.add))
                lk(dve.tensor_copy(glast[:, c, :].unsqueeze(2), blocks(gpre[:, c, :])[:, :, LB - 1:LB]))
                dve.wait_ge(proj_out, Q_ + c + 1)
                lk(dve.tensor_tensor(gpre[:, c, :], gpre[:, c, :], proj[:, Q_ + c, :], ALU.mult))
                dve.tensor_tensor(dsuf[:, c, :], dsuf[:, c, :], k, ALU.mult).then_inc(hg_kd, 1)
            def mask_values(tb):
                n, nb = tok_n(tb), nblk(tb)
                dve.wait_ge(hg_tok, tb + 1)
                for c in range(2):
                    for a2 in range(2):
                        v = kvtok[0:n, tb % 2, 256 + 64 * (2 * c + a2):256 + 64 * (2 * c + a2) + 64]
                        ins = dve.tensor_tensor(vmask[c][0:n, a2, 0:nb, :], v.unsqueeze(1).to_broadcast([n, nb, HD]),
                                                blockmask[0:n, 0:nb].unsqueeze(2).to_broadcast([n, nb, HD]), ALU.mult)
                    ins.then_inc(hg_vm, 1)

            mask_values(0)
            for tb in range(TB):
                n, nb = tok_n(tb), nblk(tb)
                if tb >= 2:
                    dve.wait_ge(hg_inter, tb - 1)
                first = states[:, tb % 2, :, 0, :]
                if tb == 0:
                    lk(dve.memset(first, 0.0))
                elif tb == TB - 1:
                    dve.wait_ge(cache_in, CACHE_HG)
                    lk(dve.tensor_copy(first, hgs0[:]))
                else:
                    lk(dve.tensor_copy(first, states[:, (tb - 1) % 2, :, 8, :]))
                dve.wait_ge(hg_upd, 2 * tb + 2)
                for b in range(nb):
                    if b:
                        dve.wait_ge(dve_step, steps[0] - 1)
                    for c in range(2):
                        ins = dve.scalar_tensor_tensor(out=states[:, tb % 2, c, b + 1, :], in0=states[:, tb % 2, c, b, :],
                                                       scalar=glast[:, c, 8 * tb + b:8 * tb + b + 1], in1=ps[:, 6 + c, HD * b:HD * b + HD],
                                                       op0=ALU.mult, op1=ALU.add)
                        if b == nb - 1 and c == 1:
                            ins.then_inc(hg_state, 1)
                        else:
                            ins.then_inc(dve_step, 1)
                            steps[0] += 1
                            if c == 0 and b:
                                dve.wait_ge(dve_step, steps[0] - 1)
                dve.wait_ge(dve_step, steps[0])
                dve.wait_ge(hg_state, tb + 1)
                if tb + 1 < TB:
                    mask_values(tb + 1)
                dve.wait_ge(hg_inter, tb + 1)
                dve.tensor_copy(of[:, 2:4, 128 * tb:128 * tb + n], ps[:, 5, 0:256].rearrange("p (c t) -> p c t", c=2)[:, :, 0:n]).then_inc(hg_inter_in, 1)
            dve.wait_ge(hg_inter_in, TB)

            def take(s_):
                d, c = divmod(s_, 2)
                dve.wait_ge(hg_att, s_ + 1)
                att = ps[:, 4 + 2 * c:6 + 2 * c, 0:NBLK // 2 * (LB - d)].rearrange("p f (b t) -> p f b t", t=LB - d)
                v = proj[:, V_ + c, :].rearrange("p (f b t) -> p f b t", f=2, t=LB)[:, :, :, 0:LB - d]
                pr = rstd[:, 0:NBLK * (LB - d)]
                ins = dve.tensor_tensor(pr.rearrange("p (f b t) -> p f b t", f=2, t=LB - d), att, v, ALU.mult)
                ins.then_inc(hg_acc, 1)
                dve.wait_ge(hg_acc, s_ + 1)
                ov = blocks(of[:, 2 + c, :])[:, :, d:LB]
                ins = dve.tensor_tensor(ov, ov, pr.rearrange("p (b t) -> p b t", t=LB - d), ALU.add)
                if d == LB - 1:
                    ins.then_inc(hg_o, 1)
                    dve.wait_ge(hg_o, c + 1)
                else:
                    lk(ins)

            for s_ in range(2 * LB):
                d, c = divmod(s_, 2)
                w = sq[:, c, 0:NBLK * (LB - d)].rearrange("p (b t) -> p b t", t=LB - d)
                q = blocks(proj[:, Q_ + c, :])[:, :, d:LB]
                if d:
                    lk(dve.tensor_tensor(q, q, blocks(proj[:, F_ + c, :])[:, :, 1:LB + 1 - d], ALU.mult))
                if s_ >= 2:
                    dve.wait_ge(hg_att, s_ - 1)
                dve.tensor_tensor(w, q, blocks(kgate[:, c, :])[:, :, 0:LB - d], ALU.mult).then_inc(hg_w, 1)
                if s_:
                    take(s_ - 1)
            take(2 * LB - 1)
            for c in range(2):
                dve.wait_ge(hg_std, c + 1)
                lk(dve.reciprocal(rstd[:], (std, sqsum)[c][:]))
                x = of[:, 2 + c, :]
                lk(dve.scalar_tensor_tensor(out=x, in0=x, scalar=par[:, R_HGN:R_HGN + 1], in1=rstd[:], op0=ALU.mult, op1=ALU.mult))
                dve.tensor_tensor(x, x, proj[:, G_ + c, :], ALU.mult).then_inc(hg_done, 1)
            dve.wait_ge(hg_done, 2)

        def pe_conv(pe):
            pe.wait_ge(cache_in, CACHE_SHORT)
            pe.wait_ge(hg_std, 2)
            for c in range(2):
                ins = pe.transpose(ps[:, 4, HIST * c:HIST * c + HIST], chist[0:HIST, 128 * c:128 * c + 128], ident[0:HIST, 0:HIST])
            ins.then_inc(cv_hist, 1)
            pe_kept_gate(pe, 0, 0)
            pe.wait_ge(cv_z, 2)
            for q, (c, t0) in enumerate(((0, SEQ), (1, SEQ), (0, ZW - HIST), (1, ZW - HIST))):
                ins = pe.transpose(ps[0:HIST, 6, 128 * q:128 * q + 128], zc[:, c, t0:t0 + HIST], ident[:])
            ins.then_inc(cv_tail, 1)
            for g in range(1, GATES_CONV):
                pe_kept_gate(pe, g, g % 2)
            pe.wait_ge(cv_y, 2)
            for t0, t1, y0 in ((0, SEQ, 0), (SEQ, T, SEQ + HIST)):
                for c in range(2):
                    ins = pe.matmul(flat(2)[:, t0:t1], ones[:], yc[:, c, y0:y0 + t1 - t0], start=c == 0, stop=c == 1)
            ins.then_inc(cv_mean, 1)
            pe.wait_ge(cv_sq, 2)
            pe.wait_ge(cv_out, 1)
            for t0, t1 in ((0, SEQ), (SEQ, T)):
                for c in range(2):
                    ins = pe.matmul(flat(3)[:, t0:t1], ones[:], sq[:, c, t0:t1], start=c == 0, stop=c == 1)
            ins.then_inc(cv_var, 1)

        GATES_CONV, GATES_SW = 10, 12

        def pe_kept_gate(pe, g, p):
            i = U0_GATE + g
            split_ready(pe, i)
            if g == 0:
                pe.wait_ge(proj_out, NPROJ)
            else:
                pe.wait_ge(gate_out, g - 1 if g < GATES_CONV else g)
            products(pe, i % SPLIT, u_hi, u_lo, range(KD), 0, p, True, True).then_inc(unit_done, 1)

        def act_kept_gate(act, g, p):
            act.wait_ge(unit_done, done(U0_GATE + g))
            if g == 0:
                act.wait_ge(hg_done, 2)
            if g == CA_:
                act.wait_ge(cv_z, 2)
            if g == SQ_:
                act.wait_ge(sw_score, len(SW))
            act.activation(halves(gkeep[:, g, :]), pair(p), ACT.Sigmoid).then_inc(gate_out, 1)

        def act_conv(act, L):
            act_kept_gate(act, 0, 0)
            act.wait_ge(cv_tail, 1)
            act.activation(ctail[0:HIST].rearrange("p q c -> p (q c)"), ps[0:HIST, 6, :], ACT.Copy).then_inc(cv_out, 1)
            act.wait_ge(cv_out, 1)
            act.dma_start(o["conv_prompt"][bass.ds(L, 1), 0].rearrange("l t (q c) -> t (l q) c", q=2), ctail[0:HIST, 0:2, :]).then_inc(outs, 16)
            act.dma_start(o["conv_sample"][bass.ds(L, 1), 0].rearrange("l t (q c) -> t (l q) c", q=2), ctail[0:HIST, 2:4, :]).then_inc(outs, 16)
            for g in range(1, GATES_CONV):
                act_kept_gate(act, g, g % 2)
            for c in range(2):
                act.wait_ge(cv_xc, c + 1)
                act.activation(sq[:, c, :], xc[:, c, :], ACT.Square).then_inc(cv_sq, 1)
            act.wait_ge(cv_var, 1)
            act.activation(std[:], flat(3), ACT.Sqrt, bias=eps_col[:], scale=1.0 / 256).then_inc(cv_std, 1)
            for c in range(2):
                act.wait_ge(cv_norm, c + 1)
                act.activation(of[:, c, :], xc[:, c, :], ACT.Silu, bias=par[:, R_LNB + c:R_LNB + c + 1]).then_inc(cv_out, 1)

        def dve_conv(dve):
            lk = lambda ins: link(dve, ins)
            lk(dve.memset(zc[:, :, 0:HIST], 0.0))
            dve.wait_ge(cv_hist, 1)
            lk(dve.tensor_copy(zc[:, :, HIST + SEQ:HIST + SEQ + HIST], ps[:, 4, 0:2 * HIST].rearrange("p (c t) -> p c t", c=2)))
            for c in range(2):
                dve.wait_ge(proj_out, CB_ + c + 1)
                ca, cb = proj[:, CA_ + c, :], proj[:, CB_ + c, :]
                lk(dve.tensor_tensor(zc[:, c, HIST:HIST + SEQ], ca[:, 0:SEQ], cb[:, 0:SEQ], ALU.mult))
                dve.tensor_tensor(zc[:, c, ZW - DEC:ZW], ca[:, SEQ:T], cb[:, SEQ:T], ALU.mult).then_inc(cv_z, 1)
            dve.wait_ge(cv_z, 2)
            for w in range(CW):
                for c in range(2):
                    wc = par[:, R_CONVW + 2 * w + c:R_CONVW + 2 * w + c + 1]
                    if w == 0:
                        ins = dve.tensor_scalar(yc[:, c, :], zc[:, c, 0:YW], wc, par[:, R_CONVB + c:R_CONVB + c + 1], ALU.mult, ALU.add)
                    else:
                        ins = dve.scalar_tensor_tensor(out=yc[:, c, :], in0=zc[:, c, w:w + YW], scalar=wc, in1=yc[:, c, :], op0=ALU.mult, op1=ALU.add)
                    if w < CW - 1:
                        lk(ins)
                    else:
                        ins.then_inc(cv_y, 1)
            dve.wait_ge(cv_mean, 1)
            dve.wait_ge(cv_y, 2)
            for c in range(2):
                lk(dve.scalar_tensor_tensor(out=xc[:, c, SEQ:T], in0=flat(2)[:, SEQ:T], scalar=-1.0 / 256, in1=yc[:, c, SEQ + HIST:YW], op0=ALU.mult, op1=ALU.add))
                dve.scalar_tensor_tensor(out=xc[:, c, 0:SEQ], in0=flat(2)[:, 0:SEQ], scalar=-1.0 / 256, in1=yc[:, c, 0:SEQ],
                                         op0=ALU.mult, op1=ALU.add).then_inc(cv_xc, 1)
            dve.wait_ge(cv_std, 1)
            lk(dve.reciprocal(rstd[:], std[:]))
            dve.wait_ge(cv_xc, 2)
            dve.wait_ge(cv_sq, 2)
            for c in range(2):
                dve.scalar_tensor_tensor(out=xc[:, c, :], in0=xc[:, c, :], scalar=par[:, R_LNG + c:R_LNG + c + 1], in1=rstd[:],
                                         op0=ALU.mult, op1=ALU.mult).then_inc(cv_norm, 1)

        SW = list(range(SEQ // CHUNK + 1))

        def sw_blocks(ch):
            if ch == SEQ // CHUNK:
                return [(0, 9), (1, 10), (2, ch)]
            return [(j, ch - 2 + j) for j in range(3) if ch - 2 + j >= 0]

        def pe_sw_tok(pe):
            pe.wait_ge(cv_std, 1)
            pe.transpose(ps[:, 4, 0:128], swk_c[:], ident[:])
            for b in range(9):
                pe.transpose(ps[0:64, 5 + b // 4, 128 * (b % 4):128 * (b % 4) + 128], proj[:, SV_, 64 * b:64 * b + 64], ident[:])
            pe.transpose(ps[:, 7, 128:256], proj[:, SK_, SEQ - WINDOW:SEQ], ident[:])
            pe.transpose(ps[0:64, 7, 256:384], proj[:, SK_, SEQ:T], ident[:]).then_inc(sw_turn, 1)

        def sw_scores(pe, i):
            if i == 0:
                pe.wait_ge(sw_tok, 6)
            if i:
                pe.wait_ge(sw_scaled, i)
            for v in range(2):
                hv = slice(64 * v, 64 * v + 64)
                q = q_sw[hv, i, :, :].rearrange("p g t -> p (g t)")
                if i == SEQ // CHUNK:
                    pe.matmul(ps[:, 4 + v, 0:128], q, swkT_c[hv, :], start=True, stop=True)
                    ins = pe.matmul(ps[:, 4 + v, 128:192], q, proj[hv, SK_, SEQ:T], start=True, stop=True)
                else:
                    t0 = max(0, 64 * i - WINDOW)
                    ins = pe.matmul(ps[:, 4 + v, 192 - (64 * i + 64 - t0):192], q, proj[hv, SK_, t0:64 * i + 64], start=True, stop=True)
            ins.then_inc(sw_score, 1)

        def sw_turn_p(pe, i):
            pe.wait_ge(sw_prob, i + 1)
            if i:
                pe.wait_ge(sw_pTs, i)
            for v in range(2):
                for j, _ in sw_blocks(i):
                    ins = pe.transpose(ps[0:64, 6 + v, 128 * j:128 * j + 128], sc[:, i % 2, v, 64 * j:64 * j + 64], ident[:])
            ins.then_inc(sw_pT, 1)

        def sw_values(pe, i):
            pe.wait_ge(sw_pTs, i + 1)
            if i >= 2:
                pe.wait_ge(sw_o, i - 1)
            bl = sw_blocks(i)
            for v in range(2):
                for n, (j, b) in enumerate(bl):
                    ins = pe.matmul(ps[64 * v:64 * v + 64, 2 + i % 2, 0:128], v64[0:64, b, 64 * v:64 * v + 64], pT[0:64, i % 2, v, j, :],
                                    start=n == 0, stop=n == len(bl) - 1)
            ins.then_inc(sw_pv, 1)

        def pe_sw(pe):
            g = GATES_CONV
            for i in range(len(SW) + 2):
                if i < len(SW):
                    sw_scores(pe, i)
                if 0 <= i - 1 < len(SW):
                    sw_turn_p(pe, i - 1)
                if 0 <= i - 2:
                    sw_values(pe, i - 2)
                if i in SW_GATE_AT:
                    pe_kept_gate(pe, g, 0)
                    g += 1

        SW_GATE_AT = (3, 6)

        def act_sw(act, L):
            act.wait_ge(sw_turn, 1)
            act.activation(swkT_c[:], ps[:, 4, 0:128], ACT.Copy).then_inc(sw_tok, 1)
            act.activation(v64[0:64, 0:4, :].rearrange("p b c -> p (b c)"), ps[0:64, 5, :], ACT.Copy).then_inc(sw_tok, 1)
            act.activation(v64[0:64, 4:8, :].rearrange("p b c -> p (b c)"), ps[0:64, 6, :], ACT.Copy).then_inc(sw_tok, 1)
            act.activation(v64[0:64, 8, :], ps[0:64, 7, 0:128], ACT.Copy).then_inc(sw_tok, 1)
            act.activation(swk_tok[:, 0, :], ps[:, 7, 128:256], ACT.Copy).then_inc(sw_tok, 1)
            act.activation(v64[0:64, 9:11, :], swv_c[0:64], ACT.Copy)
            act.activation(swk_tok[0:64, 1, :], ps[0:64, 7, 256:384], ACT.Copy).then_inc(sw_tok, 1)
            act.wait_ge(sw_tok, 6)

            def out(name, t0, n, src):
                x = o[name][bass.ds(L, 1), 0, t0:t0 + n].rearrange("l t h d -> (l t) (h d)")
                if len(src.shape) == 3:
                    x = x.rearrange("(b p) c -> p b c", p=64)
                act.dma_start(x, src).then_inc(outs, 16)

            out("swa_k_prompt", 0, 128, swk_tok[:, 0, :])
            out("swa_v_prompt", 0, 128, v64[0:64, 6:8, :])
            out("swa_k_sample", 0, 64, swk_c[64:128, :])
            out("swa_k_sample", 64, 64, swk_tok[0:64, 1, :])
            out("swa_v_sample", 0, 64, swv_c[0:64, 1, :])
            out("swa_v_sample", 64, 64, v64[0:64, 8, :])

            g = GATES_CONV
            for i in range(len(SW) + 2):
                if i < len(SW):
                    k0 = 64 * sw_blocks(i)[0][0]
                    st = stat[:, i % 2]
                    act.wait_ge(sw_max, i + 1)
                    for v in range(2):
                        x = sc[:, i % 2, v, k0:192]
                        act.activation(x, x, ACT.Exp, bias=st[:, 1, v:v + 1], accum_out=st[:, 3, v:v + 1])
                    act.activation(st[:, 4, :], st[:, 2, :], ACT.Exp).then_inc(sw_exp, 1)
                if 1 <= i <= len(SW):
                    j0 = sw_blocks(i - 1)[0][0]
                    act.wait_ge(sw_pT, i)
                    if i >= 3:
                        act.wait_ge(sw_pv, i - 2)
                    act.activation(pT[0:64, (i - 1) % 2, :, j0:3, :].rearrange("p v j q -> p v (j q)"), ps[0:64, 6:8, 128 * j0:384], ACT.Copy).then_inc(sw_pTs, 1)
                if i >= 2:
                    act.wait_ge(sw_pv, i - 1)
                    act.activation(of[:, 4:6, 64 * (i - 2):64 * (i - 2) + 64], ps[:, 2 + i % 2, 0:128].rearrange("p (g q) -> p g q", g=2), ACT.Copy).then_inc(sw_o, 1)
                if i in SW_GATE_AT:
                    act_kept_gate(act, g, 0)
                    g += 1

        def dve_sw(dve):
            lk = lambda ins: link(dve, ins)

            def prob(i):
                k0 = 64 * sw_blocks(i)[0][0]
                x, st = sc[:, i % 2, :, k0:192], stat[:, i % 2]
                dve.wait_ge(sw_exp, i + 1)
                lk(dve.tensor_tensor(st[:, 5, :], st[:, 3, :], st[:, 4, :], ALU.add))
                lk(dve.reciprocal(st[:, 5, :], st[:, 5, :]))
                dve.tensor_tensor(x, x, st[:, 5, :].unsqueeze(2).to_broadcast([128, 2, 192 - k0]), ALU.mult).then_inc(sw_prob, 1)

            for i in SW:
                k0 = 64 * sw_blocks(i)[0][0]
                x, st = sc[:, i % 2, :, k0:192], stat[:, i % 2]
                if i >= 2:
                    dve.wait_ge(sw_pT, i - 1)
                dve.wait_ge(sw_score, i + 1)
                dve.scalar_tensor_tensor(out=x, in0=ps[:, 4:6, k0:192], scalar=HD ** -0.5, in1=alibi[:, :, k0:192], op0=ALU.mult, op1=ALU.add).then_inc(sw_scaled, 1)
                dve.wait_ge(sw_scaled, i + 1)
                lk(dve.tensor_reduce(st[:, 0, :], x, AX.X, ALU.max))
                lk(dve.tensor_tensor(st[:, 0, :], st[:, 0, :], sinkcol[:], ALU.max))
                lk(dve.tensor_scalar(st[:, 1, :], st[:, 0, :], -1.0, None, ALU.mult))
                dve.tensor_tensor(st[:, 2, :], sinkcol[:], st[:, 1, :], ALU.add).then_inc(sw_max, 1)
                if i:
                    prob(i - 1)
            prob(len(SW) - 1)

        SB = [(hd, kb) for hd in range(4) for kb in (3, 2, 1, 0)] + [(None, kb) for kb in (None, 3, 2, 1, 0)]

        def sb_shape(i):
            hd, kb = SB[i]
            if hd is None:
                return (64 if kb is None else 128), 4 * DEC
            return 128, SEQ - 128 * kb

        def sb_first(i):
            return i == 0 or SB[i][0] != SB[i - 1][0]

        def sb_diagonal(i):
            hd, kb = SB[i]
            return hd is not None or kb is None

        def sb_sums(i):
            return sum(SB[j][1] != 0 for j in range(i + 1))

        def pe_sb_tok(pe):
            pe.wait_ge(sw_o, len(SW))
            pe.wait_ge(cache_in, CACHE_SB)
            for tb in range(TB):
                if tb >= 2:
                    pe.wait_ge(sb_tok, tb - 1)
                for q, x in enumerate((BK_, BK_ + 1, BV_, BV_ + 1)):
                    n = tok_n(tb)
                    ins = pe.transpose(ps[0:n, 4 + tb % 2, 128 * q:128 * q + 128], proj[:, x, 128 * tb:128 * tb + n], ident[:])
                ins.then_inc(sb_turn, 1)
            for c in range(2):
                for kb in range(4):
                    ins = pe.transpose(ps[:, 6 + c, 128 * kb:128 * kb + 128], sbk_c[:, kb, 128 * c:128 * c + 128], ident[:])
                ins.then_inc(sb_turn, 1)

        def sb_logits(pe, i):
            hd, kb = SB[i]
            bk = 4 + i % 2
            if i == 0:
                pe.wait_ge(sb_tok, TB + 2)
            if i >= 2:
                pe.wait_ge(sb_min, i - 1)
            if hd is not None:
                hh, c = slice(64 * (hd % 2), 64 * (hd % 2) + 64), hd // 2
                pe.matmul(ps[:, bk, 0:SEQ - 128 * kb], proj[hh, BK_ + c, 128 * kb:128 * kb + 128], proj[hh, BQ_ + c, 128 * kb:SEQ],
                          start=True, stop=True).then_inc(sb_z, 1)
                return
            for q in (0, 2, 1, 3):
                hh, c = slice(64 * (q % 2), 64 * (q % 2) + 64), q // 2
                if q == 1:
                    pe.wait_ge(sb_zrow, i - 4 * 4 + 1)
                k = proj[hh, BK_ + c, SEQ:T] if kb is None else sbkT_c[hh, c, 128 * kb:128 * kb + 128]
                ins = pe.matmul(ps[0:sb_shape(i)[0], bk, 64 * q:64 * q + 64], k, proj[hh, BQ_ + c, SEQ:T],
                                start=q == 0, stop=q == 3, skip_group_check=True)
                if q == 2:
                    ins.then_inc(sb_zrow, 1)
            ins.then_inc(sb_z, 1)

        def sb_rest(pe, i):
            nk, w = sb_shape(i)
            bk = 4 + i % 2
            pe.wait_ge(sb_sp, i + 1)
            ins = pe.matmul(ps[0:nk, bk, 0:w], trineg[0:nk, 0:nk], spx[0:nk, i % 2, 0:w], start=False, stop=sb_first(i), skip_group_check=True)
            if not sb_first(i):
                q0, z0 = (0, 0) if SB[i][0] is None else (128 * SB[i][1] + 128, 128)
                pe.wait_ge(sb_sum, sb_sums(i - 1))
                ins = pe.matmul(ps[:, bk, z0:w], negones[:], sqsum[:, q0:q0 + w - z0], start=False, stop=True, skip_group_check=True)
            ins.then_inc(sb_arg, 1)

        def sb_values(pe, i):
            hd, kb = SB[i]
            nk, w = sb_shape(i)
            if sb_diagonal(i):
                pe.wait_ge(sb_a, sum(sb_diagonal(j) for j in range(i + 1)))
            else:
                pe.wait_ge(sb_exp, i + 1)
            if hd is not None:
                if sb_first(i) and hd >= 2:
                    pe.wait_ge(sb_o, hd - 1)
                hh = slice(64 * (hd % 2), 64 * (hd % 2) + 64)
                pe.matmul(ps[hh, 6 + hd % 2, 128 * kb:SEQ], sbtok[:, kb, 256 + 64 * hd:256 + 64 * hd + 64], arg[:, i % 2, 0:w],
                          start=sb_first(i), stop=kb == 0, skip_group_check=True).then_inc(sb_pv, 1)
                return
            for q in range(4):
                hh, c = slice(64 * (q % 2), 64 * (q % 2) + 64), q // 2
                v = sbtok[0:64, TB - 1, 256 + 64 * q:256 + 64 * q + 64] if kb is None else sbv_c[:, kb, 64 * q:64 * q + 64]
                ins = pe.matmul(ps[hh, 2, 64 * c:64 * c + 64], v, arg[0:nk, i % 2, 64 * q:64 * q + 64],
                                start=sb_first(i) and c == 0, stop=kb == 0, skip_group_check=True)
            ins.then_inc(sb_pv, 1)

        def pe_sb(pe):
            for i in range(len(SB) + 2):
                if i < len(SB):
                    sb_logits(pe, i)
                if 0 <= i - 1 < len(SB):
                    sb_rest(pe, i - 1)
                if i >= 2:
                    sb_values(pe, i - 2)
                if i in SB_GATE_AT:
                    pe_kept_gate(pe, GATES_SW + SB_GATE_AT.index(i), 0)

        SB_GATE_AT = (2, 7, 12, 17)

        def act_sb(act, L):
            def out(name, t0, n, src):
                x = o[name][bass.ds(L, 1), 0, t0:t0 + n].rearrange("l t h d -> (l t) (h d)")
                if len(src.shape) == 3:
                    x = x.rearrange("(b p) c -> p b c", p=128)
                act.dma_start(x, src).then_inc(outs, 16)

            for tb in range(TB):
                act.wait_ge(sb_turn, tb + 1)
                act.activation(sbtok[0:tok_n(tb), tb, :], ps[0:tok_n(tb), 4 + tb % 2, :], ACT.Copy).then_inc(sb_tok, 1)
            for c in range(2):
                act.wait_ge(sb_turn, TB + c + 1)
                act.activation(sbkT_c[:, c, :], ps[:, 6 + c, :], ACT.Copy).then_inc(sb_tok, 1)
            act.wait_ge(sb_tok, TB)
            out("sb_k_prompt", 0, SEQ, sbtok[:, 0:4, 0:256])
            out("sb_v_prompt", 0, SEQ, sbtok[:, 0:4, 256:512])
            out("sb_k_sample", 0, DEC, sbtok[0:64, 4, 0:256])
            out("sb_v_sample", 0, DEC, sbtok[0:64, 4, 256:512])

            def evac(i):
                hd, kb = SB[i]
                if kb == 0:
                    act.wait_ge(sb_pv, i + 1)
                    if hd is None:
                        act.activation(of[:, 6:8, SEQ:T], ps[:, 2, 0:128].rearrange("p (c q) -> p c q", c=2), ACT.Copy).then_inc(sb_o, 1)
                    else:
                        hh = slice(64 * (hd % 2), 64 * (hd % 2) + 64)
                        act.activation(of[hh, 6 + hd // 2, 0:SEQ], ps[hh, 6 + hd % 2, :], ACT.Copy).then_inc(sb_o, 1)

            for i in range(len(SB) + 2):
                if i < len(SB):
                    nk, w = sb_shape(i)
                    x = sq[0:nk, i % 2, 0:w]
                    act.wait_ge(sb_z, i + 1)
                    if i >= 2:
                        act.wait_ge(sb_sp, i - 1)
                    act_link(act, act.activation(x, ps[0:nk, 4 + i % 2, 0:w], ACT.Abs))
                    act_link(act, act.activation(x, x, ACT.Exp, scale=-1.0))
                    act.activation(x, x, ACT.Ln, bias=ones[0:nk, 0:1]).then_inc(sb_ln, 1)
                if 0 <= i - 1 < len(SB):
                    nk, w = sb_shape(i - 1)
                    x = arg[0:nk, (i - 1) % 2, 0:w]
                    act.wait_ge(sb_min, i)
                    act.activation(x, x, ACT.Exp).then_inc(sb_exp, 1)
                if i >= 2:
                    evac(i - 2)
                if i in SB_GATE_AT:
                    act_kept_gate(act, GATES_SW + SB_GATE_AT.index(i), 0)

        def dve_sb(dve):
            lk = lambda ins: link(dve, ins)

            def mask(i, x):
                if SB[i][0] is None:
                    v = x[0:64, i % 2, 0:256].rearrange("p (h q) -> p h q", h=4)
                    return dve.tensor_tensor(v, v, later[0:64, 0:64].unsqueeze(1).to_broadcast([64, 4, 64]), ALU.mult)
                return dve.tensor_tensor(x[:, i % 2, 0:128], x[:, i % 2, 0:128], later[:], ALU.mult)

            def finish(i):
                hd, kb = SB[i]
                nk, w = sb_shape(i)
                dve.wait_ge(sb_arg, i + 1)
                if i >= 2:
                    dve.wait_ge(sb_pv, i - 1)
                dve.tensor_scalar(arg[0:nk, i % 2, 0:w], ps[0:nk, 4 + i % 2, 0:w], 0.0, None, ALU.min).then_inc(sb_min, 1)
                if kb != 0:
                    if hd is None:
                        if kb is None:
                            lk(dve.memset(sqsum[:, 0:w], 0.0))
                        ins = dve.tensor_tensor(sqsum[0:nk, 0:w], sqsum[0:nk, 0:w], spx[0:nk, i % 2, 0:w], ALU.add)
                    else:
                        q0 = 128 * kb
                        if not sb_first(i):
                            lk(dve.tensor_tensor(sqsum[:, q0 + 128:SEQ], sqsum[:, q0 + 128:SEQ], spx[:, i % 2, 128:w], ALU.add))
                        ins = dve.tensor_copy(sqsum[:, q0:q0 + 128], spx[:, i % 2, 0:128])
                    ins.then_inc(sb_sum, 1)
                    dve.wait_ge(sb_sum, sb_sums(i))
                if sb_diagonal(i):
                    dve.wait_ge(sb_exp, i + 1)
                    mask(i, arg).then_inc(sb_a, 1)

            for i in range(len(SB)):
                nk, w = sb_shape(i)
                z = ps[0:nk, 4 + i % 2, 0:w]
                if i:
                    finish(i - 1)
                dve.wait_ge(sb_ln, i + 1)
                ins = dve.scalar_tensor_tensor(out=spx[0:nk, i % 2, 0:w], in0=z, scalar=0.0, in1=sq[0:nk, i % 2, 0:w], op0=ALU.max, op1=ALU.add)
                if sb_diagonal(i):
                    lk(ins)
                    ins = mask(i, spx)
                ins.then_inc(sb_sp, 1)
            finish(len(SB) - 1)

        def pe_gates(pe):
            with pe.Fori(0, 2) as it:
                for m in range(4):
                    u0 = U0_PAIR + 3 * m
                    i = it * 12 + u0
                    split_ready(pe, i)
                    pe.wait_ge(sig_done, it * 8 + (2 * m + 1))
                    if m == 0:
                        pe.wait_ge(gate_out, 2 * KD)
                    for n in range(NB):
                        if m == 0:
                            pe.wait_ge(o_ready, 2 * n + 2)
                        ins = products(pe, u0 % SPLIT, o_hi, o_lo, (2 * n, 2 * n + 1), 2 * n, n, True, True)
                    ins.then_inc(unit_done, 1)
                    for n in (2, 3):
                        split_ready(pe, i + (n - 1))
                        pe.wait_ge(yb_out, it * 16 + (4 * m + n + 1))
                        products(pe, (u0 + n - 1) % SPLIT, u_hi, u_lo, range(KD), 0, n, True, True).then_inc(unit_done, 1)

        def pe_out(pe):
            for m in range(KD):
                i = U0_OUT + m
                split_ready(pe, i)
                if m == 0:
                    pe.wait_ge(m_ready, KD)
                if m >= 4:
                    pe.wait_ge(y_ready, y_before[N_MPOST] + m + 1)
                products(pe, i % SPLIT, m_split[:, :, 0, :], m_split[:, :, 1, :], range(KD), 0, m % 4, True, True).then_inc(unit_done, 1)
            pe_norm(pe, N_MPOST, 0)

        def act_gates(act):
            for m in range(KD):
                u0 = U0_PAIR + 3 * m
                act.wait_ge(unit_done, done(u0))
                if m:
                    act.wait_ge(gated, 4 * m)
                for n in range(NB):
                    act.activation(halves(ybr[:, n, :]), pair(n), ACT.Copy).then_inc(yb_out, 1)
                for n in (2, 3):
                    act.wait_ge(unit_done, done(u0 + n - 1))
                    act.activation(halves(sg[:, n - 2, :]), pair(n), ACT.Sigmoid).then_inc(sig_done, 1)

        def dve_gates(dve):
            for m in range(KD):
                for n in range(NB):
                    if n < 2:
                        dve.wait_ge(yb_out, 4 * m + n + 1)
                        if m == 0:
                            dve.wait_ge(gate_out, n + 15)
                    else:
                        dve.wait_ge(sig_done, 2 * m + n)
                    gate = gkeep[:, 2 * m + n, :] if n < 2 else sg[:, n - 2, :]
                    dst = mprod[:, n % 2, :] if n else msum[:]
                    if m and n == 0:
                        dve.wait_ge(m_ready, m)
                    dve.tensor_tensor(dst, gate, ybr[:, n, :], ALU.mult).then_inc(gated, 1)
                    if n:
                        dve.wait_ge(gated, 4 * m + n + 1)
                        link(dve, dve.tensor_tensor(msum[:], msum[:], dst, ALU.add))
                link(dve, dve.tensor_copy(m_split[:, m, 0, :], msum[:]))
                dve.tensor_tensor(m_split[:, m, 1, :], msum[:], m_split[:, m, 0, :], ALU.subtract).then_inc(m_ready, 1)

        def pe_mixer(pe):
            pe_norm(pe, N_MPRE, 0)
            for t in range(CA_):
                pe_proj(pe, t)
            hg_turn(pe, 0)
            for tb in range(TB):
                hg_update(pe, tb, 0)
                hg_update(pe, tb, 1)
                if tb + 1 < TB:
                    hg_turn(pe, tb + 1)
                pe_proj(pe, CA_ + tb)
                hg_states_out(pe, tb)
            t = CA_ + TB
            for s_ in range(2 * LB):
                hg_distance(pe, s_)
                if s_ % 3 == 2 and t < NPROJ:
                    pe_proj(pe, t)
                    t += 1
            for c in range(2):
                hg_norm_pe(pe, c)
            assert t == NPROJ
            pe_conv(pe)
            pe_sw_tok(pe)
            pe_sw(pe)
            pe_sb_tok(pe)
            pe_sb(pe)
            pe_gates(pe)
            pe_out(pe)

        def act_mixer(act, L):
            act_norm_h(act, N_MPRE)
            act.wait_ge(u_ready, 16)
            act.dma_start(chist[0:HIST, :], a["cache_conv"][bass.ds(L, 1), 0].rearrange("l t c -> (l t) c")).then_inc(cache_in, 16)
            act.dma_start(swk_c[:], a["cache_swa_k"][bass.ds(L, 1), 0].rearrange("l t h d -> (l t) (h d)")).then_inc(cache_in, 16)
            act.dma_start(swv_c[0:64], a["cache_swa_v"][bass.ds(L, 1), 0].rearrange("l (b p) h d -> p (l b) (h d)", p=64)).then_inc(cache_in, 16)
            act_proj_some(act, CA_)
            act_hg(act)
            act_proj_some(act, NPROJ - CA_ - TB)
            act_hg_out(act, L)
            act_hg_norm(act)
            act.wait_ge(outs, 32)
            act.wait_ge(hg_inter, TB)
            act.dma_start(sbk_c[:], a["cache_sb_k"][bass.ds(L, 1), 0].rearrange("l (b p) h d -> p (l b) (h d)", p=128)).then_inc(cache_in, 16)
            act.dma_start(sbv_c[:], a["cache_sb_v"][bass.ds(L, 1), 0].rearrange("l (b p) h d -> p (l b) (h d)", p=128)).then_inc(cache_in, 16)
            act_conv(act, L)
            act.wait_ge(cv_out, 3)
            act_sw(act, L)
            act.wait_ge(outs, 64 + 96)
            act.preload_act_table_set("natural_log_exp_and_others")
            act_sb(act, L)
            act.wait_ge(outs, 64 + 96 + 64)
            act.wait_ge(sb_o, 5)
            for t in range(2 * NB):
                act.activation(o_hi[:, t, :], of[:, t, :], ACT.Copy).then_inc(o_high, 1)
            act_gates(act)
            for m in range(KD):
                act_y(act, N_MPOST, m, U0_OUT + m, m % 4)
            act_root(act, N_MPOST, 0)

        def dve_mixer(dve, L):
            dve_apply(dve, N_MPRE)
            layer[0] = L
            dve_hg(dve)
            dve.wait_ge(hg_std, 2)
            dve_conv(dve)
            dve.wait_ge(sw_tok, 6)
            dve_sw(dve)
            dve_sb(dve)
            for t in range(2 * NB):
                dve.wait_ge(o_high, t + 1)
                dve.tensor_tensor(o_lo[:, t, :], of[:, t, :], o_hi[:, t, :], ALU.subtract).then_inc(o_ready, 1)
            dve_gates(dve)
            for m in range(KD):
                dve_add_square(dve, N_MPOST, m)
            dve_residual(dve, N_MPOST, y)

        def pe_ple(pe):
            pe.wait_ge(tok_ple, 32)
            pe.wait_ge(y_ready, 4 + y_before[N_F2POST] + KD)
            for c in range(2):
                for tb in range(TB):
                    n = tok_n(tb)
                    ins = pe.transpose(flat(2 + c)[:, 128 * tb:128 * tb + n], ptok[0:n, tb, 128 * c:128 * c + 128], ident[0:n, 0:n])
                ins.then_inc(p_turned, 1)
            for q in range(2):
                i = U0_PLEW + q
                split_ready(pe, i)
                pe.wait_ge(p_ready, 2)
                for m in range(4):
                    if q:
                        pe.wait_ge(e_out, m + 1)
                    for kk in range(2):
                        for c, (wt, x) in enumerate(((whi, p_hi), (whi, p_lo), (wlo, p_hi))):
                            for f in range(2):
                                ins = pe.matmul(ps[:, 2 * m + f, 0:HT], wt[:, i % SPLIT, 512 * kk + 128 * m:512 * kk + 128 * m + 128],
                                                x[:, kk, HT * f:HT * f + HT], start=kk == 0 and c == 0, stop=kk == 1 and c == 2, skip_group_check=True)
                ins.then_inc(unit_done, 1)
            pe.wait_ge(e_out, KD)
            pe_norm(pe, N_PPRE, 0)
            for m in range(KD):
                i = U0_PLEG + m
                split_ready(pe, i)
                if m == 0:
                    pe.wait_ge(u_ready, 32)
                if m >= 4:
                    pe.wait_ge(ple_sig, m - 3)
                products(pe, i % SPLIT, u_hi, u_lo, range(KD), 0, m % 4, True, True).then_inc(unit_done, 1)
            pe_norm(pe, N_PPOST, 0)

        def act_ple(act, L):
            act.dma_start(ptok[:, 0:4, :], a["p_prompt"][bass.ds(L, 1), 0].rearrange("l (b p) c -> p (l b) c", p=128)).then_inc(tok_ple, 16)
            act.dma_start(ptok[0:DEC, 4, :], a["p_sample"][bass.ds(L, 1), 0].rearrange("l t c -> (l t) c")).then_inc(tok_ple, 16)
            for c in range(2):
                act.wait_ge(p_turned, c + 1)
                act_link(act, act.activation(pf[:, c, :], flat(2 + c), ACT.Copy))
                act.activation(p_hi[:, c, :], pf[:, c, :], ACT.Copy).then_inc(p_high, 1)
            for m in range(KD):
                act.wait_ge(unit_done, done(U0_PLEW + m // 4))
                act.activation(halves(e[:, m, :]), pair(m % 4), ACT.Copy).then_inc(e_out, 1)
            act_norm_h(act, N_PPRE)
            for m in range(KD):
                act.wait_ge(unit_done, done(U0_PLEG + m))
                if m >= 2:
                    act.wait_ge(e_gated, m - 1)
                act.activation(halves(gsig[:, m % 2, :]), pair(m % 4), ACT.Sigmoid).then_inc(ple_sig, 1)
                act.wait_ge(e_gated, m + 1)
                act_square(act, N_PPOST, m, e[:, m, :])
            act_root(act, N_PPOST, 0)

        def dve_ple(dve):
            for c in range(2):
                dve.wait_ge(p_high, c + 1)
                dve.tensor_tensor(p_lo[:, c, :], pf[:, c, :], p_hi[:, c, :], ALU.subtract).then_inc(p_ready, 1)
            dve_residual(dve, N_F2POST, y)
            dve_apply(dve, N_PPRE)
            for m in range(KD):
                dve.wait_ge(ple_sig, m + 1)
                dve.wait_ge(e_out, m + 1)
                dve.tensor_tensor(e[:, m, :], e[:, m, :], gsig[:, m % 2, :], ALU.mult).then_inc(e_gated, 1)
                if m:
                    dve_add_square(dve, N_PPOST, m - 1)
            dve_add_square(dve, N_PPOST, KD - 1)
            dve_residual(dve, N_PPOST, e)

        GAIN_NAMES = ["ffn1_pre_g", "ffn1_post_g", "mix_pre_g", "mix_post_g", "ffn2_pre_g", "ffn2_post_g", "ple_pre_g", "ple_post_g"]
        with nc.Fori(0, DEPTH) as L:
            with nc.Block() as block:

                @block.sync
                def _(sp_):
                    load_ffn(sp_, L, a["ffn1_up"], a["ffn1_down"], U0_FFN1)
                    for t in range(NPROJ):
                        i = U0_PROJ + t
                        slot = i % RAW
                        if t in (SQ_, SQ_ + 1):
                            for v in range(2):
                                c = C_SQ + 128 * v + 64 * (t - SQ_)
                                if v == 0:
                                    sp_.wait_ge(w_split, i + 1)
                                sp_.dma_start(wraw[:, slot, :].rearrange("p (k n) -> p k n", k=KD)[:, :, 64 * v:64 * v + 64],
                                              cols(a["w_in"], L, slice(c, c + 64))).then_inc(w_loaded[slot], 16)
                            continue
                        if t in (SK_, SV_):
                            c = C_SK if t == SK_ else C_SV
                        else:
                            g = max(x for x in PROJ_COL if x <= t)
                            c = PROJ_COL[g] + 128 * (t - g)
                        load_unit(sp_, slot, i, cols(a["w_in"], L, slice(c, c + 128)))
                    wb = a["w_branch"].rearrange("l n r c -> l (n r) c")
                    for g in range(2 * KD):
                        cg = C_GATE + D * (g % 2) + 128 * (g // 2)
                        load_unit(sp_, (U0_GATE + g) % RAW, U0_GATE + g, cols(a["w_in"], L, slice(cg, cg + 128)))
                    for m in range(KD):
                        i = U0_PAIR + 3 * m
                        slot, c = i % RAW, slice(128 * m, 128 * m + 128)
                        sp_.wait_ge(w_split, i + 1)
                        v = wraw[:, slot, :].rearrange("p (k n) -> p k n", k=8)
                        sp_.dma_start(v[:, 0:4, :], cols(wb, L, c, 0, 4)).then_inc(w_loaded[slot], 16)
                        for kv in range(2):
                            sp_.dma_start(v[64 * kv:64 * kv + 64, 4:6, :],
                                          wb[bass.ds(L, 1), 512 + 128 * kv:640 + 128 * kv, c].rearrange("l (g d) n -> d (l g) n", g=2)).then_inc(w_loaded[slot], 16)
                        sp_.dma_start(v[:, 6:8, :], cols(wb, L, c, 6, 2)).then_inc(w_loaded[slot], 16)
                        for n in (2, 3):
                            cg = C_GATE + D * n + 128 * m
                            load_unit(sp_, (i + n - 1) % RAW, i + n - 1, cols(a["w_in"], L, slice(cg, cg + 128)))
                    for m in range(KD):
                        i = U0_OUT + m
                        load_unit(sp_, i % RAW, i, cols(a["w_out"], L, slice(128 * m, 128 * m + 128)))
                    load_ffn(sp_, L, a["ffn2_up"], a["ffn2_down"], U0_FFN2)
                    for q in range(2):
                        i = U0_PLEW + q
                        sp_.wait_ge(w_split, i + 1)
                        sp_.dma_start(wraw[:, i % RAW, :].rearrange("p (k n) -> p k n", k=2),
                                      a["ple_w"][bass.ds(L, 1), :, 512 * q:512 * q + 512].rearrange("l (k p) n -> p (l k) n", p=128)).then_inc(w_loaded[i % RAW], 16)
                    for m in range(KD):
                        i = U0_PLEG + m
                        load_unit(sp_, i % RAW, i, cols(a["ple_gate_w"], L, slice(128 * m, 128 * m + 128)))

                @block.gpsimd
                def _(pool):
                    pool.sem_inc(w_split, RAW)
                    landed = [0] * RAW

                    def split(slot, i, i_part, n_landed):
                        pool.wait_ge(w_loaded[slot], n_landed)
                        pool.wait_ge(unit_done, i + 1)
                        pool.tensor_tensor(whi[:, i_part, :], wraw[:, slot, :], ones[:, 0:1].to_broadcast([128, 1024]), ALU.mult).then_inc(w_rounded, 1)
                        pool.wait_ge(w_rounded, i + 1)
                        pool.tensor_tensor(wlo[:, i_part, :], wraw[:, slot, :], whi[:, i_part, :], ALU.subtract).then_inc(w_split, 1)

                    def split_run(i0, i1):
                        assert (i1 - i0) % RAW == 0
                        with pool.Fori(0, (i1 - i0) // RAW) as it:
                            for q in range(RAW):
                                slot = (i0 + q) % RAW
                                split(slot, it * RAW + (i0 + q), (i0 + q) % SPLIT, it * 16 + (landed[slot] + 16))
                        for q in range(RAW):
                            landed[q] += 16 * (i1 - i0) // RAW

                    def split_one(i, dmas):
                        landed[i % RAW] += 16 * dmas
                        split(i % RAW, i, i % SPLIT, landed[i % RAW])

                    split_run(0, U0_PROJ)
                    for i in range(U0_PROJ, U0_OUT + 2):
                        branch = U0_PAIR <= i < U0_OUT and (i - U0_PAIR) % 3 == 0
                        swq = i - U0_PROJ in (SQ_, SQ_ + 1)
                        split_one(i, 4 if branch else 2 if swq else 1)
                    split_run(U0_OUT + 2, UNITS)

                @block.tensor
                def _(pe):
                    pe.sem_inc(unit_done, SPLIT)
                    pe.wait_ge(par_loaded, 15 * 16)
                    pe.transpose(ps[:, 7, 0:64], prow[0:64, 0, :], ident[0:64, 0:64])
                    pe.transpose(ps[:, 7, 64:64 + NROW2], prow[0:NROW2, 1, :], ident[0:NROW2, 0:NROW2]).then_inc(par_turned, 1)
                    pe_ffn(pe, 0, U0_FFN1)
                    pe_mixer(pe)
                    pe_ffn(pe, 1, U0_FFN2)
                    pe_ple(pe)

                @block.scalar
                def _(act):
                    act.sem_inc(y_ready, 4)
                    act.sem_inc(sig_done, 1)
                    for n, name in enumerate(GAIN_NAMES):
                        act.dma_start(prow[8 * n:8 * n + 8, 0, :], a[name][bass.ds(L, 1), :].rearrange("l (k p) -> (l k) p", p=128)).then_inc(par_loaded, 16)
                    act.dma_start(prow[R_CONVW:R_CONVW + 62, 1, :], a["conv_w"][bass.ds(L, 1)].rearrange("l w (c p) -> (l w c) p", p=128)).then_inc(par_loaded, 16)
                    for r, name in ((R_CONVB, "conv_b"), (R_LNG, "conv_ln_g"), (R_LNB, "conv_ln_b")):
                        act.dma_start(prow[r:r + 2, 1, :], a[name][bass.ds(L, 1), :].rearrange("l (c p) -> (l c) p", p=128)).then_inc(par_loaded, 16)
                    for a2 in range(2):
                        act.dma_start(prow[R_HGN:R_HGN + 1, 1, 64 * a2:64 * a2 + 64], a["hgrn_norm_g"][bass.ds(L, 1), :]).then_inc(par_loaded, 16)
                    act.dma_start(sink4[:], a["swa_sinks"][bass.ds(L, 1), :].to_broadcast([128, 4])).then_inc(par_loaded, 16)
                    act.dma_start(hgs0[:], a["state_hgrn"][bass.ds(L, 1), 0].rearrange("l (c a) k v -> (a k) (l c) v", a=2)).then_inc(cache_in, 16)
                    act.wait_ge(par_turned, 1)
                    for n0, n1, scale in ((0, 1, 1.0), (1, 2, 0.5), (2, 5, 1.0), (5, 6, 0.5), (6, 8, 1.0)):
                        act.activation(gains[:, 8 * n0:8 * n1], ps[:, 7, 8 * n0:8 * n1], ACT.Copy, scale=scale).then_inc(par_ready, 1)
                    act.activation(par[:], ps[:, 7, 64:64 + NROW2], ACT.Copy).then_inc(par_ready, 1)
                    for g in range(2):
                        hg2 = slice(64 * g, 64 * g + 64)
                        act.activation(sinkcol[hg2, :].unsqueeze(2), sink4[hg2, :].rearrange("p (v g) -> p v g", g=2)[:, :, g:g + 1], ACT.Copy).then_inc(par_ready, 1)
                    act_ffn(act, 0, U0_FFN1)
                    act_mixer(act, L)
                    act_ffn(act, 1, U0_FFN2)
                    act_ple(act, L)
                    act.wait_ge(outs, 16 * N_OUTS)

                @block.vector
                def _(dve):
                    dve.sem_inc(up_mul, 2)
                    dve.sem_inc(s_ready, 2)
                    dve.wait_ge(par_ready, 8)
                    for k in range(KD):
                        dve_add_square(dve, N_F1PRE, k)
                    dve_ffn(dve, 0, U0_FFN1)
                    dve_residual(dve, N_F1POST, y)
                    dve_mixer(dve, L)
                    dve_ffn(dve, 1, U0_FFN2)
                    dve_ple(dve)

            with nc.Block() as block:

                @block.vector
                def _(dve):
                    for x in per_layer:
                        dve.sem_clear(x)

        with nc.Block() as block:

            @block.tensor
            def _(pe):
                for t in range(TB):
                    n = tok_n(t)
                    if t >= 4:
                        pe.wait_ge(placed, n_placed[0] + t - 3)
                    for k in range(KD):
                        ins = pe.transpose(ps[0:n, 2 * (t % 4) + k // 4, 128 * (k % 4):128 * (k % 4) + 128], h[:, k, 128 * t:128 * t + n], ident[:])
                    ins.then_inc(turned, 1)

            @block.vector
            def _(dve):
                for t in range(TB):
                    n = tok_n(t)
                    dve.wait_ge(turned, KD + 2 + t + 1)
                    dve.tensor_copy(xtok[0:n, t, :], ps[0:n, 2 * (t % 4):2 * (t % 4) + 2, :].rearrange("p a n -> p (a n)")).then_inc(placed, 1)

            @block.sync
            def _(sp_):
                for t in range(TB):
                    n = tok_n(t)
                    sp_.wait_ge(placed, n_placed[0] + t + 1)
                    dst = o["y_prompt"][0, 128 * t:128 * t + 128, :] if t < 4 else o["y_sample"][0]
                    sp_.dma_start(dst, xtok[0:n, t, :]).then_inc(out_tok, 16)
                sp_.wait_ge(out_tok, 16 * TB)


OUTS = [
    ("y_prompt", (1, SEQ, D)), ("y_sample", (1, DEC, D)),
    ("conv_prompt", (DEPTH, 1, HIST, 256)), ("conv_sample", (DEPTH, 1, HIST, 256)),
    ("hgrn_prompt", (DEPTH, 1, 4, HD, HD)), ("hgrn_sample", (DEPTH, 1, 4, HD, HD)),
    ("swa_k_prompt", (DEPTH, 1, WINDOW, 2, HD)), ("swa_v_prompt", (DEPTH, 1, WINDOW, 2, HD)),
    ("swa_k_sample", (DEPTH, 1, WINDOW, 2, HD)), ("swa_v_sample", (DEPTH, 1, WINDOW, 2, HD)),
    ("sb_k_prompt", (DEPTH, 1, SEQ, 4, HD)), ("sb_v_prompt", (DEPTH, 1, SEQ, 4, HD)),
    ("sb_k_sample", (DEPTH, 1, DEC, 4, HD)), ("sb_v_sample", (DEPTH, 1, DEC, 4, HD)),
]


def kernel(**inputs):
    import numpy as np
    import concourse.bacc as bacc
    from concourse.bass_utils import run_bass_kernel_spmd

    nc = bacc.Bacc("TRN2", target_bir_lowering=False, num_devices=1)
    arrays, a = {}, {}
    for name, x in inputs.items():
        x = np.ascontiguousarray(x)
        arrays[f"in_{name}"] = x
        a[name] = nc.dram_tensor(f"in_{name}", x.shape, mybir.dt.from_np(x.dtype), kind="ExternalInput").ap()
    o = {name: nc.dram_tensor(f"out_{name}", shape, F32, kind="ExternalOutput").ap() for name, shape in OUTS}
    trunk(nc, a, o)
    r = run_bass_kernel_spmd(nc, [arrays], core_ids=[0])
    return tuple(r.results[0][f"out_{name}"] for name, _ in OUTS)
```

```python
from contextlib import ExitStack

import concourse.bass as bass
from concourse import mybir

F32 = mybir.dt.float32
F32R = mybir.dt.float32r
ALU = mybir.AluOpType
ACT = mybir.ActivationFunctionType
AX = mybir.AxisListType

D = 1024
SEQ, DEC = 512, 64
T = SEQ + DEC
HT = T // 2
DEPTH = 2
CHUNK = 64
EPS = 1e-6
FF = 2816
PLE = 256
NB = 4
CW = 31
HIST = CW - 1
WINDOW = 128
HD = 64
KD = D // 128
KF = FF // 128
LB = 16
NBLK = T // LB
TB = (T + 127) // 128
SLOPES = [2.0 ** (-8.0 * (h + 1) / 4) for h in range(4)]

C_CA, C_CB, C_HQ, C_HF, C_HI, C_HG = 0, 256, 512, 768, 1024, 1280
C_SQ, C_SK, C_SV, C_BQ, C_BK, C_BV, C_GATE = 1536, 1792, 1920, 2048, 2304, 2560, 2816
F_, Q_, V_, G_, CA_, CB_, SQ_, SK_, SV_, BQ_, BK_, BV_ = 0, 2, 4, 6, 8, 10, 12, 14, 15, 16, 18, 20
NPROJ = 22
PROJ_COL = {F_: C_HF, Q_: C_HQ, V_: C_HI, G_: C_HG, CA_: C_CA, CB_: C_CB, BQ_: C_BQ, BK_: C_BK, BV_: C_BV}

U_UP, U_DOWN = 2 * KF, 3 * KD
U_FFN = U_UP + U_DOWN
U0_FFN1 = 0
U0_PROJ = U_FFN
U0_GATE = U0_PROJ + NPROJ
U0_PAIR = U0_GATE + 2 * KD
U0_OUT = U0_GATE + 5 * KD
U0_FFN2 = U0_OUT + KD
U0_PLEW = U0_FFN2 + U_FFN
U0_PLEG = U0_PLEW + 2
UNITS = U0_PLEG + KD
RAW = 4
SPLIT = 2
DOWN_K = [(0, 8), (8, 16), (16, KF)]

ROOT_SET = "sqrt_and_others"
EXP_LN_SET = "natural_log_exp_and_others"
N_F1PRE, N_F1POST, N_MPRE, N_MPOST, N_F2PRE, N_F2POST, N_PPRE, N_PPOST = range(8)
R_CONVB, R_LNG, R_LNB = range(3)
N_TAPS = DEPTH * CW * 2
N_ROWS = 9 * DEPTH
N_ROW_LOADS = 16
GAIN_NAMES = ["ffn1_pre_g", "ffn1_post_g", "mix_pre_g", "mix_post_g", "ffn2_pre_g", "ffn2_post_g", "ple_pre_g", "ple_post_g"]


def trunk(nc, a, o):
    n_consts = [0]
    n_placed = [0]
    with ExitStack() as ctx:
        base = nc.sbuf_base
        arena = ctx.enter_context(nc.sbuf_tensor("arena", [128, (nc.sbuf_usable_end - base) // 4 - 16], F32))
        limit = nc.sbuf_usable_end

        class Region:

            def __init__(self, at):
                self.at = at

            def __call__(self, name, shape, dt=F32, parts=128):
                n = 4
                for s in shape:
                    n *= s
                at = (self.at + 31) // 32 * 32
                self.at = at + n
                assert self.at <= limit, (name, self.at, limit)
                return nc.alloc_sbuf_tensor_at(name, [parts, *shape], dt, offset=at)

        def sem(name):
            return ctx.enter_context(nc.semaphore(name))

        keep = Region((base + 31) // 32 * 32)
        h = keep("h", [KD, T])
        wraw = keep("wraw", [RAW, 1024])
        whi = keep("whi", [SPLIT, 1024], F32R)
        wlo = keep("wlo", [SPLIT, 1024], F32R)
        ident = keep("ident", [128])
        ones = keep("ones", [128])
        headones = keep("headones", [128])
        trineg = keep("trineg", [128])
        negones = keep("negones", [128])
        later = keep("later", [128])
        blockmask = keep("blockmask", [8])
        alibi = keep("alibi", [2, WINDOW + CHUNK])
        blockend = keep("blockend", [T])
        eps_col = keep("eps_col", [1])
        gains = keep("gains", [64])
        taps = keep("taps", [CW, 2])
        crow = keep("crow", [3, 2])
        hgn = keep("hgn", [1])
        gains_all = keep("gains_all", [8, DEPTH, 8])
        taps_all = keep("taps_all", [DEPTH, 2 * CW])
        rows_all = keep("rows_all", [7 * DEPTH])
        sinks_all = keep("sinks_all", [DEPTH, 2, 2])
        lb_all = keep("lb_all", [DEPTH, 2])
        lb = keep("lb", [2])
        lb1m = keep("lb1m", [2])
        sinkcol = keep("sinkcol", [2])
        sq = keep("sq", [2, T])
        sqsum = keep("sqsum", [T])
        roots = keep("roots", [2 * T])
        std, rstd = roots[:, 0:T], roots[:, T:2 * T]
        rcol = keep("rcol", [TB])
        diag = roots[:, 0:TB * 128].rearrange("p (t n) -> p t n", t=TB)

        u_at = keep.at
        ru = Region(u_at)
        u_hi = ru("u_hi", [KD, T], F32R)
        u_lo = ru("u_lo", [KD, T], F32R)
        y = Region(u_at)("y", [KD, T])
        rf = Region(ru.at)
        s_hi = rf("s_hi", [KF, T], F32R)
        s_lo = rf("s_lo", [KF, T], F32R)
        uf = Region(ru.at)("uf", [KD, T])
        silu_a = sq

        rm = Region(ru.at)
        rcache = Region(ru.at)
        chist = rcache("chist", [256])
        ctail = rcache("ctail", [4, 128])
        swk_c = rcache("swk_c", [128])
        swv_c = rcache("swv_c", [2, 128])
        rm("caches", [2, T])
        proj_at = rm.at
        proj = rm("proj", [NPROJ, T])
        of = rm("of", [2 * NB, T])
        tmp_at = rm.at
        rh = Region(tmp_at)
        kgate = rh("kgate", [2, T])
        gpre = rh("gpre", [2, T])
        dsuf = rh("dsuf", [2, T])
        kvtok = of[:, 4:6, :].rearrange("p a n -> p (a n)")[:, 0:1024].rearrange("p (a c) -> p a c", a=2)
        vmask = [rh("vmask", [2, 8, HD]), sq[:].rearrange("p a n -> p (a n)")[:, 0:16 * HD].rearrange("p (a b v) -> p a b v", a=2, b=8)]
        states = rh("states", [2, 2, 9, HD])
        hgs0 = rh("hgs0", [2, HD])
        glast = sqsum[:, 0:2 * NBLK].rearrange("p (c b) -> p c b", c=2)
        rc = Region(tmp_at)
        ZW = HIST + SEQ + HIST + DEC
        YW = ZW - HIST
        zc = rc("zc", [2, ZW])
        yc = rc("yc", [2, YW])
        xc = rc("xc", [2, T])
        rs = Region(tmp_at)
        swkT_c = rs("swkT_c", [128])
        v64 = rs("v64", [11, 128])
        swk_tok = rs("swk_tok", [2, 128])
        sc = rs("sc", [2, 2, 192])
        pT = rs("pT", [2, 2, 3, 128])
        stat = rs("stat", [2, 6, 2])
        rbc = Region(limit - 8192 - 32)
        sbk_c = rbc("sbk_c", [4, 256])
        sbv_c = rbc("sbv_c", [4, 256])
        assert rs.at <= limit - 8224
        rb = Region(tmp_at)
        sbkT_c = rb("sbkT_c", [2, SEQ])
        sbtok = rb("sbtok", [TB, 512])
        spx = rb("spx", [2, 512])
        arg = rb("arg", [2, 512])
        gkeep = proj
        m_split = Region(proj_at)("m_split", [KD, 2, T], F32R)
        ro = Region(proj_at + 16 * T * 4)
        ybr = ro("ybr", [NB, T])
        sg = ro("sg", [2, T])
        assert ro.at <= proj_at + NPROJ * T * 4
        o_lo = Region(proj_at + NPROJ * T * 4)("o_lo", [2 * NB, T], F32R)
        rq = Region(tmp_at)
        o_hi = rq("o_hi", [2 * NB, T], F32R)
        mprod = rq("mprod", [2, T])
        msum = rq("msum", [T])
        rp = Region(ru.at)
        rp("normed", [KD, T])
        e = rp("e", [KD, T])
        gsig = rp("gsig", [2, T])
        rpt = Region(u_at + KD * T * 4)
        ptok = rpt("ptok", [TB, PLE])
        p_hi = rpt("p_hi", [2, T], F32R)
        p_lo = rpt("p_lo", [2, T], F32R)
        assert rpt.at <= ru.at
        rr = Region(ru.at)
        prow = rr("prow", [3, 128])
        prow_end = rr.at
        xtok = Region(prow_end)("xtok", [TB, D])

        ps = ctx.enter_context(nc.psum_tensor("ps", [128, 8, 512], F32))

        def pair(p):
            return ps[:, 2 * p:2 * p + 2, 0:HT]

        def flat(p):
            return ps[:, 2 * p:2 * p + 2, :].rearrange("p a n -> p (a n)")[:, 0:T]

        def halves(ap):
            return ap.rearrange("p (a n) -> p a n", a=2)

        consts_done = sem("consts_done")
        tok_loaded = sem("tok_loaded")
        x_loaded = [sem(f"x_loaded{c}") for c in range(4)]
        rows_loaded = sem("rows_loaded")
        turned = sem("turned")
        placed = sem("placed")
        out_tok = sem("out_tok")
        w_loaded = [sem(f"w_loaded{i}") for i in range(RAW)]
        w_rounded = sem("w_rounded")
        w_split = sem("w_split")
        unit_done = sem("unit_done")
        par_ready = sem("par_ready")
        sq_ready = sem("sq_ready")
        sq_added = sem("sq_added")
        norm_sum = sem("norm_sum")
        std_ready = sem("std_ready")
        diag_ready = sem("diag_ready")
        factors_out = sem("factors_out")
        y_normed = sem("y_normed")
        h_ready = sem("h_ready")
        h_ready_pool = sem("h_ready_pool")
        u_full = sem("u_full")
        u_high = sem("u_high")
        u_ready = sem("u_ready")
        u_ready_pool = sem("u_ready_pool")
        silu_done = sem("silu_done")
        up_mul = sem("up_mul")
        s_high = sem("s_high")
        s_ready = sem("s_ready")
        y_ready = sem("y_ready")
        dve_step = sem("dve_step")
        act_step = sem("act_step")
        proj_out = sem("proj_out")
        cache_in = sem("cache_in")
        outs = sem("outs")
        hg_kd = sem("hg_kd")
        hg_turned = sem("hg_turned")
        hg_tok = sem("hg_tok")
        hg_vm = sem("hg_vm")
        hg_upd = sem("hg_upd")
        hg_state = sem("hg_state")
        hg_inter = sem("hg_inter")
        hg_inter_in = sem("hg_inter_in")
        hg_w = sem("hg_w")
        hg_att = sem("hg_att")
        hg_acc = sem("hg_acc")
        hg_o = sem("hg_o")
        hg_done = sem("hg_done")
        gate_out = sem("gate_out")
        gate_sig = sem("gate_sig")
        hg_sq = sem("hg_sq")
        hg_ss = sem("hg_ss")
        hg_std = sem("hg_std")
        cv_hist = sem("cv_hist")
        cv_z = sem("cv_z")
        cv_y = sem("cv_y")
        cv_mean = sem("cv_mean")
        cv_xc = sem("cv_xc")
        cv_sq = sem("cv_sq")
        cv_var = sem("cv_var")
        cv_std = sem("cv_std")
        cv_norm = sem("cv_norm")
        cv_tail = sem("cv_tail")
        cv_out = sem("cv_out")
        sw_turn = sem("sw_turn")
        sw_tok = sem("sw_tok")
        sw_score = sem("sw_score")
        sw_scaled = sem("sw_scaled")
        sw_max = sem("sw_max")
        sw_exp = sem("sw_exp")
        sw_prob = sem("sw_prob")
        sw_pT = sem("sw_pT")
        sw_pTs = sem("sw_pTs")
        sw_pv = sem("sw_pv")
        sw_o = sem("sw_o")
        sb_turn = sem("sb_turn")
        sb_tok = sem("sb_tok")
        sb_z = sem("sb_z")
        sb_zrow = sem("sb_zrow")
        sb_ln = sem("sb_ln")
        sb_sp = sem("sb_sp")
        sb_arg = sem("sb_arg")
        sb_sum = sem("sb_sum")
        sb_min = sem("sb_min")
        sb_exp = sem("sb_exp")
        sb_a = sem("sb_a")
        sb_pv = sem("sb_pv")
        sb_o = sem("sb_o")
        o_high = sem("o_high")
        o_ready = sem("o_ready")
        yb_out = sem("yb_out")
        sig_done = sem("sig_done")
        gated = sem("gated")
        m_ready = sem("m_ready")
        p_turned = sem("p_turned")
        p_high = sem("p_high")
        p_ready = sem("p_ready")
        tok_ple = sem("tok_ple")
        ple_sig = sem("ple_sig")
        e_gated = sem("e_gated")
        e_made = sem("e_made")
        e_out = sem("e_out")
        per_layer = [x for x in locals().values() if isinstance(x, bass.SemaphoreHandle)]
        per_layer = [x for x in per_layer if x not in (consts_done, tok_loaded, rows_loaded, turned, placed, out_tok)] + w_loaded

        with nc.Block() as block:
            NT = SEQ // 128

            @block.sync
            def _(sp_):
                sp_.dma_start(xtok[0:DEC, NT, :], a["x_sample"][0]).then_inc(tok_loaded, 16)
                for c in range(4):
                    f = slice(D // 4 * c, D // 4 * (c + 1))
                    sp_.dma_start(xtok[:, 0:NT, f], a["x_prompt"][0].rearrange("(t p) d -> p t d", p=128)[:, :, f]).then_inc(x_loaded[c], 16)

            @block.gpsimd
            def _(pool):
                n = [0]

                def link(ins):
                    n[0] += 1
                    ins.then_inc(consts_done, 1)
                    pool.wait_ge(consts_done, n[0])

                link(pool.memset(ident[:], 0.0))
                link(pool.affine_select(out=ident[:], in_=ident[:], compare_op=ALU.not_equal, fill=1.0, base=0,
                                        pattern=[[-1, 128]], channel_multiplier=1))
                link(pool.memset(ones[:], 1.0))
                link(pool.memset(negones[:], -1.0))
                link(pool.memset(eps_col[:], EPS))
                link(pool.memset(headones[:], 0.0))
                link(pool.memset(headones[0:64, 0:64], 1.0))
                link(pool.memset(headones[64:128, 64:128], 1.0))
                link(pool.affine_select(out=trineg[:], in_=negones[:], compare_op=ALU.is_ge, fill=0.0, base=0,
                                        pattern=[[-1, 128]], channel_multiplier=1))
                link(pool.affine_select(out=later[:], in_=ones[:], compare_op=ALU.is_gt, fill=0.0, base=0,
                                        pattern=[[1, 128]], channel_multiplier=-1))
                link(pool.affine_select(out=blockmask[:], in_=ones[:, 0:8], compare_op=ALU.is_ge, fill=0.0, base=0,
                                        pattern=[[-LB, 8]], channel_multiplier=1))
                link(pool.affine_select(out=blockmask[:], in_=blockmask[:], compare_op=ALU.is_ge, fill=0.0, base=LB - 1,
                                        pattern=[[LB, 8]], channel_multiplier=-1))
                link(pool.memset(blockend[:], 0.0))
                link(pool.memset(blockend[:].rearrange("p (b t) -> p b t", t=LB)[:, :, LB - 1:LB], 1.0))
                for g in range(2):
                    half = slice(64 * g, 64 * g + 64)
                    for v in range(2):
                        link(pool.iota(alibi[half, v, :], pattern=[[-1, WINDOW + CHUNK]], base=WINDOW, channel_multiplier=1,
                                       allow_small_or_imprecise_dtypes=True))
                        neg = wraw[half, v, 0:WINDOW + CHUNK]
                        link(pool.tensor_scalar(neg, alibi[half, v, :], 0.0, SLOPES[2 * v + g], ALU.min, ALU.mult))
                        link(pool.tensor_scalar(alibi[half, v, :], alibi[half, v, :], 0.0, -SLOPES[2 * v + g], ALU.max, ALU.mult))
                        link(pool.tensor_tensor(alibi[half, v, :], alibi[half, v, :], neg, ALU.add))
                n_consts[0] = n[0]

            @block.tensor
            def _(pe):
                pe.wait_ge(consts_done, 2)
                pe.wait_ge(tok_loaded, 16)
                for k in range(KD):
                    if k % 2 == 0:
                        pe.wait_ge(x_loaded[k // 2], 16)
                    if k >= 4:
                        pe.wait_ge(placed, k - 3)
                    for t in range(TB):
                        n = min(128, T - 128 * t)
                        ins = pe.transpose(flat(k % 4)[:, 128 * t:128 * t + n], xtok[0:n, t, 128 * k:128 * k + 128], ident[0:n, 0:n])
                    ins.then_inc(turned, 1)
                pe.wait_ge(placed, KD)
                pe.wait_ge(rows_loaded, 16 * N_ROW_LOADS)
                for q, n in enumerate((128, N_TAPS, N_ROWS)):
                    ins = pe.transpose(ps[:, q, 0:n], prow[0:n, q, :], ident[0:n, 0:n])
                ins.then_inc(turned, 1)

            @block.vector
            def _(dve):
                for k in range(KD):
                    dve.wait_ge(turned, k + 1)
                    dve.tensor_copy(h[:, k, :], flat(k % 4)).then_inc(placed, 1)
                dve.wait_ge(turned, KD + 1)
                n = [KD]

                def link(ins):
                    n[0] += 1
                    ins.then_inc(placed, 1)
                    dve.wait_ge(placed, n[0])

                lg, mx, sm = std[:, 0:4], std[:, 4:6], std[:, 6:8]
                link(dve.tensor_copy(lg, ps[:, 2, N_ROWS - 4:N_ROWS]))
                link(dve.tensor_tensor(mx, lg[:, 0:2], lg[:, 2:4], ALU.max))
                link(dve.tensor_tensor(lg[:, 0:2], lg[:, 0:2], mx, ALU.subtract))
                link(dve.tensor_tensor(lg[:, 2:4], lg[:, 2:4], mx, ALU.subtract))
                link(dve.tensor_copy(gains_all[:].rearrange("p n l k -> p (n l k)"), ps[:, 0, 0:128]))
                for q in (N_F1POST, N_F2POST):
                    g = gains_all[:, q, :, :]
                    link(dve.tensor_scalar(g, g, 0.5, None, ALU.mult))
                link(dve.tensor_copy(taps_all[:].rearrange("p l w -> p (l w)"), ps[:, 1, 0:N_TAPS]))
                link(dve.tensor_copy(rows_all[:, 0:N_ROWS - 4], ps[:, 2, 0:N_ROWS - 4]))
                dve.wait_ge(turned, KD + 2)
                link(dve.tensor_tensor(sm, lg[:, 0:2], lg[:, 2:4], ALU.add))
                link(dve.reciprocal(sm, sm))
                link(dve.tensor_tensor(lg[:, 0:2], lg[:, 0:2], sm, ALU.mult))
                link(dve.tensor_tensor(lg[:, 2:4], lg[:, 2:4], sm, ALU.mult))
                link(dve.tensor_tensor(lb_all[:, 0, :], lg[:, 0:2], lg[:, 0:2], ALU.subtract))
                link(dve.tensor_tensor(lb_all[:, 1, :], lg[:, 0:2], lg[:, 2:4], ALU.add))
                link(dve.tensor_tensor(lb_all[:, 1, :], lb_all[:, 1, :], lg[:, 0:2], ALU.subtract))
                n_placed[0] = n[0]

            @block.scalar
            def _(act):
                for n, name in enumerate(GAIN_NAMES):
                    act.dma_start(prow[8 * DEPTH * n:8 * DEPTH * (n + 1), 0, :], a[name].rearrange("l (k p) -> (l k) p", p=128)).then_inc(rows_loaded, 16)
                act.dma_start(prow[0:N_TAPS, 1, :], a["conv_w"].rearrange("l w (c p) -> (l w c) p", p=128)).then_inc(rows_loaded, 16)
                for r, name in ((R_CONVB, "conv_b"), (R_LNG, "conv_ln_g"), (R_LNB, "conv_ln_b")):
                    act.dma_start(prow[2 * DEPTH * r:2 * DEPTH * (r + 1), 2, :], a[name].rearrange("l (c p) -> (l c) p", p=128)).then_inc(rows_loaded, 16)
                for half in range(2):
                    act.dma_start(prow[6 * DEPTH:7 * DEPTH, 2, 64 * half:64 * half + 64], a["hgrn_norm_g"]).then_inc(rows_loaded, 16)
                act.dma_start(prow[7 * DEPTH:9 * DEPTH, 2, :], a["hgrn_lb_logits"].rearrange("l (c p) -> (l c) p", p=128)).then_inc(rows_loaded, 16)
                act.dma_start(sinks_all[:].rearrange("p l v g -> p (l v g)"),
                              a["swa_sinks"].rearrange("(o l) h -> o (l h)", o=1).to_broadcast([128, 4 * DEPTH])).then_inc(rows_loaded, 16)
                act.wait_ge(placed, KD + 4)
                act.activation(std[:, 0:4], std[:, 0:4], ACT.Exp).then_inc(turned, 1)

        def done(i):
            return i + 1 + SPLIT

        def load_unit(sp_, slot, i, src, n=8):
            sp_.wait_ge(w_split, i + 1)
            sp_.dma_start(wraw[:, slot, 0:128 * n].rearrange("p (k n) -> p k n", k=n), src).then_inc(w_loaded[slot], 16)

        def cols(w, L, c, k0=0, nk=8):
            v = w[bass.ds(L, 1), 128 * k0:128 * (k0 + nk), c].rearrange("l (k p) n -> p (l k) n", p=128)
            return v

        def load_ffn(sp_, L, up, down, u0):
            with sp_.Fori(0, KF // 2) as it:
                for q in range(4):
                    c = bass.ds(it * 256 + 128 * (q // 2) + FF * (q % 2), 128)
                    load_unit(sp_, (u0 + q) % RAW, it * 4 + (u0 + q), cols(up, L, c))
            with sp_.Fori(0, 2) as it:
                for m in range(4):
                    for q, (k0, k1) in enumerate(DOWN_K):
                        i = U_UP + 3 * m + q
                        load_unit(sp_, (u0 + i) % RAW, it * 12 + (u0 + i), cols(down, L, bass.ds(it * 512 + 128 * m, 128), k0, k1 - k0), k1 - k0)

        def products(pe, part, x_hi, x_lo, ks, k_off, p, start, stop, wait_k=None):
            ins = None
            for n, k in enumerate(ks):
                if wait_k is not None:
                    wait_k(k)
                w = slice(128 * (k_off + n), 128 * (k_off + n) + 128)
                for c, (wt, x) in enumerate(((whi, x_hi), (whi, x_lo), (wlo, x_hi))):
                    for f in range(2):
                        ins = pe.matmul(ps[:, 2 * p + f, 0:HT], wt[:, part, w], x[:, k, HT * f:HT * f + HT],
                                        start=start and n == 0 and c == 0, stop=stop and n == len(ks) - 1 and c == 2,
                                        skip_group_check=True)
            return ins

        def split_ready(pe, i):
            pe.wait_ge(w_split, i + 1 + RAW)

        def ones_product(pe, p, w, x, start=True, stop=True):
            for f in range(2):
                ins = pe.matmul(ps[:, 2 * p + f, 0:HT], w, x[:, HT * f:HT * f + HT], start=start, stop=stop)
            return ins

        def keep_clock(pe, n):
            for _ in range(n):
                pe.matmul(ps[:, 1, 0:128], ones[:], ident[:], start=True, stop=True)

        def token_sums(pe, x, start, stop, same=1):
            for tb in range(TB):
                t0 = min(128 * tb, T - 128)
                ins = pe.matmul(ps[:, 0, SAME * tb:SAME * tb + same], x[:, t0:t0 + 128], ones[:, 0:same], start=start and tb == 0,
                                stop=stop and tb == TB - 1, skip_group_check=True)
            return ins

        SAME = 64

        def pe_broadcast(pe, n):
            keep_clock(pe, 3)
            pe.wait_ge(diag_ready, n + 1)
            pe.matmul(flat(3)[:, 0:SEQ], ones[:], roots[:, 0:SEQ], start=True, stop=True)
            pe.matmul(flat(3)[:, SEQ:T], ones[:], roots[:, SEQ + 64:SEQ + 128], start=True, stop=True).then_inc(factors_out, 1)

        def pe_norm_y(pe, n):
            keep_clock(pe, 4)
            pe.wait_ge(sq_added, 8 * n + 8)
            token_sums(pe, sqsum, True, True).then_inc(norm_sum, 1)
            pe_broadcast(pe, n)
            if n != N_F2POST:
                keep_clock(pe, 14)

        def pe_norm_h(pe, n):
            for k in range(KD):
                pe.wait_ge(sq_ready, 8 * n + k + 1)
                token_sums(pe, sq[:, k % 2, :], k == 0, k == KD - 1, SAME).then_inc(sq_added, 1)
            pe_broadcast(pe, n)
            keep_clock(pe, 6)

        def u_tile_ready(pe, n):
            def wait(k):
                if k in LO_POOL:
                    pe.wait_ge(u_ready_pool, len(LO_POOL) * (n // 2) + LO_POOL.index(k) + 1)
                else:
                    pe.wait_ge(u_ready, len(LO_DVE) * (n // 2) + LO_DVE.index(k) + 1)
            return wait

        def pe_ffn(pe, f, u0):
            if f == 0:
                keep_clock(pe, 14)
                pe_norm_y(pe, N_F1PRE)
            else:
                pe_norm_h(pe, N_F2PRE)
            with pe.Fori(0, KF // 2) as it:
                for q in range(4):
                    i = it * 4 + (u0 + q)
                    split_ready(pe, i)
                    pe.wait_ge(up_mul, it * 2 + (f * KF + q // 2 + 1))
                    products(pe, (u0 + q) % SPLIT, u_hi, u_lo, range(KD), 0, q, True, True,
                             wait_k=u_tile_ready(pe, 4 * f + N_F1PRE) if q == 0 else None).then_inc(unit_done, 1)
            with pe.Fori(0, 2) as it:
                for m in range(4):
                    for q, (k0, k1) in enumerate(DOWN_K):
                        i = it * 12 + (u0 + U_UP + 3 * m + q)
                        split_ready(pe, i)
                        if q == 0:
                            pe.wait_ge(y_ready, it * 4 + (m + 1 + y_before[4 * f + N_F1POST]))
                        if m == 0 and q != 1:
                            pe.wait_ge(s_ready, f * KF + 2 + (KF - 1 if q == 0 else KF))
                        products(pe, (u0 + U_UP + 3 * m + q) % SPLIT, s_hi, s_lo, range(k0, k1), 0, m, q == 0, q == 2).then_inc(unit_done, 1)
            if f:
                pe_turn_p(pe)
            pe.wait_ge(y_ready, 4 + y_before[4 * f + N_F1POST] + 5)
            pe_norm_y(pe, 4 * f + N_F1POST)

        y_before = {N_F1POST: 0, N_MPOST: 8, N_F2POST: 16, N_PPOST: 24}

        def act_square(act, n, k, src):
            if 8 * n + k >= 2:
                act.wait_ge(sq_added, 8 * n + k - 1)
            act.activation(sq[:, k % 2, :] if src.ndim == 2 else halves(sq[:, k % 2, :]), src, ACT.Square).then_inc(sq_ready, 1)

        def act_square_h(act, n, k):
            if n:
                if k in ADD_POOL:
                    act.wait_ge(h_ready_pool, len(ADD_POOL) * (n // 2 - 1) + ADD_POOL.index(k) + 1)
                else:
                    act.wait_ge(h_ready, len(ADD_DVE) * (n // 2 - 1) + ADD_DVE.index(k) + 1)
            act_square(act, n, k, h[:, k, :])

        def act_norm_h(act, n):
            for k in range(KD):
                act_square_h(act, n, k)
            act_norm_root(act, n)

        def act_norm_root(act, n):
            act_root(act, n)
            for k in range(KD):
                act.wait_ge(u_full, 8 * (n // 2) + k + 1)
                act.activation(u_hi[:, k, :], uf[:, k, :], ACT.Copy).then_inc(u_high, 1)

        def act_root(act, n):
            if n == N_F1PRE or n % 2:
                act.wait_ge(norm_sum, 1 + (n + 1) // 2)
            else:
                act.wait_ge(sq_added, 8 * n + 8)
            act.activation(rcol[:], ps[:, 0, 0:TB * SAME].rearrange("p (t s) -> p t s", t=TB)[:, :, 0], ACT.Sqrt, bias=eps_col[:], scale=1.0 / D).then_inc(std_ready, 1)

        def act_y(act, n, m, unit, p):
            act.wait_ge(unit_done, done(unit))
            act_square(act, n, m, pair(p))
            act.activation(halves(y[:, m, :]), pair(p), ACT.Copy).then_inc(y_ready, 1)

        def act_ffn(act, L, f, u0):
            act_norm_h(act, 4 * f + N_F1PRE)
            with act.Fori(0, KF // 2) as it:
                for q in range(2):
                    act.wait_ge(unit_done, it * 4 + done(u0 + 2 * q))
                    act.wait_ge(s_ready, it * 2 + (f * KF + q + 1))
                    act.activation(halves(silu_a[:, q, :]), pair(2 * q), ACT.Silu).then_inc(silu_done, 1)
            act.preload_act_table_set(ROOT_SET)
            if f:
                act.wait_ge(unit_done, done(u0 + U_UP - 1))
                act.dma_start(ptok[:, 0:4, :], a["p_prompt"][bass.ds(L, 1), 0].rearrange("l (b p) c -> p (l b) c", p=128)).then_inc(tok_ple, 16)
                act.dma_start(ptok[0:DEC, 4, :], a["p_sample"][bass.ds(L, 1), 0].rearrange("l t c -> (l t) c")).then_inc(tok_ple, 16)
            for m in range(KD):
                act_y(act, 4 * f + N_F1POST, m, u0 + U_UP + 3 * m + 2, m % 4)
            if f:
                act_turned_p(act)
            act_root(act, 4 * f + N_F1POST)

        steps = [0]

        def link(dve, ins):
            steps[0] += 1
            ins.then_inc(dve_step, 1)
            dve.wait_ge(dve_step, steps[0])

        def dve_add_square(dve, n, k):
            dve.wait_ge(sq_ready, 8 * n + k + 1)
            if k == 0:
                if n:
                    dve.wait_ge(norm_sum, n // 2 + 1)
                dve.tensor_copy(sqsum[:], sq[:, 0, :]).then_inc(sq_added, 1)
            else:
                dve.wait_ge(sq_added, 8 * n + k)
                dve.tensor_tensor(sqsum[:], sqsum[:], sq[:, k % 2, :], ALU.add).then_inc(sq_added, 1)

        def dve_rstd(dve, n):
            dve.wait_ge(std_ready, n + 1)
            link(dve, dve.reciprocal(rcol[:], rcol[:]))
            dve.tensor_tensor(diag, ident[:].unsqueeze(1).to_broadcast([128, TB, 128]), rcol[:].unsqueeze(2).to_broadcast([128, TB, 128]),
                              ALU.mult).then_inc(diag_ready, 1)
            dve.wait_ge(factors_out, n + 1)

        LO_POOL, LO_DVE = (1, 2, 4, 5, 6), (0, 3, 7)
        ADD_POOL, ADD_DVE = (1, 3, 4, 6), (0, 2, 5, 7)

        def low(engine, n, k, signal):
            engine.wait_ge(u_high, 8 * (n // 2) + k + 1)
            engine.tensor_tensor(u_lo[:, k, :], uf[:, k, :], u_hi[:, k, :], ALU.subtract).then_inc(signal, 1)

        def dve_apply(dve, n):
            dve_rstd(dve, n)
            for k in range(KD):
                dve.scalar_tensor_tensor(out=uf[:, k, :], in0=h[:, k, :], scalar=gains[:, 8 * n + k:8 * n + k + 1],
                                         in1=flat(3), op0=ALU.mult, op1=ALU.mult).then_inc(u_full, 1)
                if k and k - 1 in LO_DVE:
                    low(dve, n, k - 1, u_ready)
            low(dve, n, KD - 1, u_ready)

        def add_to_h(engine, n, k, signal):
            engine.wait_ge(y_normed, 8 * (n // 2) + k + 1)
            engine.tensor_tensor(h[:, k, :], h[:, k, :], uf[:, k, :], ALU.add).then_inc(signal, 1)

        def dve_residual(dve, n, src):
            dve_rstd(dve, n)
            for k in range(KD):
                if n != N_PPOST:
                    dve.wait_ge(y_ready, 4 + y_before[n] + k + 1)
                dve.scalar_tensor_tensor(out=uf[:, k, :], in0=src[:, k, :], scalar=gains[:, 8 * n + k:8 * n + k + 1],
                                         in1=flat(3), op0=ALU.mult, op1=ALU.mult).then_inc(y_normed, 1)
                if k and k - 1 in ADD_DVE:
                    add_to_h(dve, n, k - 1, h_ready)
            add_to_h(dve, n, KD - 1, h_ready)
            dve.wait_ge(h_ready, len(ADD_DVE) * (n // 2 + 1))
            dve.wait_ge(h_ready_pool, len(ADD_POOL) * (n // 2 + 1))

        def pool_apply(pool, n):
            for k in LO_POOL:
                low(pool, n, k, u_ready_pool)

        def pool_residual(pool, n):
            for k in ADD_POOL:
                add_to_h(pool, n, k, h_ready_pool)

        def dve_ffn(dve, f, u0):
            dve_apply(dve, 4 * f + N_F1PRE)
            with dve.Fori(0, KF // 2) as it:
                for q in range(2):
                    x = silu_a[:, q, :]
                    dve.wait_ge(unit_done, it * 4 + done(u0 + 2 * q + 1))
                    dve.wait_ge(silu_done, it * 2 + (f * KF + q + 1))
                    dve.tensor_tensor(halves(x), halves(x), pair(2 * q + 1), ALU.mult).then_inc(up_mul, 1)
                    dve.wait_ge(up_mul, it * 2 + (f * KF + q + 1 + 2))
                    dve.tensor_scalar(s_hi[:, bass.ds(it * 2 + q, 1), :].rearrange("p a n -> p (a n)"), x, 1.0, None, ALU.mult).then_inc(s_high, 1)
                    dve.wait_ge(s_high, it * 2 + (f * KF + q + 1))
                    dve.tensor_tensor(s_lo[:, bass.ds(it * 2 + q, 1), :].rearrange("p a n -> p (a n)"), x,
                                      s_hi[:, bass.ds(it * 2 + q, 1), :].rearrange("p a n -> p (a n)"), ALU.subtract).then_inc(s_ready, 1)
            for m in range(KD):
                dve_add_square(dve, 4 * f + N_F1POST, m)
            if f:
                dve_turned_p(dve)

        N_OUTS = 2 + 2 + 6 + 4
        CACHE_HG, CACHE_SHORT, CACHE_SB = 4 * 16, 4 * 16, 6 * 16
        asteps = [0]

        def act_link(act, ins):
            asteps[0] += 1
            ins.then_inc(act_step, 1)
            act.wait_ge(act_step, asteps[0])

        THIRDS = ((0, 3), (3, 6), (6, KD))
        QUARTERS = ((0, 2), (2, 4), (4, 6), (6, KD))
        FIFTHS = ((0, 2), (2, 4), (4, 6), (6, 7), (7, KD))

        def unit_part(pe, i, j, p, parts):
            k0, k1 = parts[j]
            ins = products(pe, i % SPLIT, u_hi, u_lo, range(k0, k1), k0, p, j == 0, j == len(parts) - 1)
            if j == len(parts) - 1:
                ins.then_inc(unit_done, 1)

        def pe_proj_free(pe, t):
            split_ready(pe, U0_PROJ + t)
            if t >= 2:
                pe.wait_ge(proj_out, t - 1)

        def pe_proj(pe, t):
            i = U0_PROJ + t
            pe_proj_free(pe, t)
            products(pe, i % SPLIT, u_hi, u_lo, range(KD), 0, t % 2, True, True,
                     wait_k=u_tile_ready(pe, N_MPRE) if t == 0 else None).then_inc(unit_done, 1)

        def pe_proj_part(pe, t, j, parts):
            if j == 0:
                pe_proj_free(pe, t)
            unit_part(pe, U0_PROJ + t, j, t % 2, parts)

        next_proj = [0]
        q_sw = proj[:, SQ_:SQ_ + 2, :].rearrange("p a n -> p (a n)").rearrange("p (c g t) -> p c g t", g=2, t=CHUNK)

        def act_proj_some(act, n):
            for t in range(next_proj[0], next_proj[0] + n):
                act.wait_ge(unit_done, done(U0_PROJ + t))
                x, y_ = halves(proj[:, t, :]), pair(t % 2)
                if t in (F_, F_ + 1):
                    act.activation(halves(kgate[:, t, :]), y_, ACT.Sigmoid, scale=-1.0)
                    ins = act.activation(x, y_, ACT.Sigmoid)
                elif t in (G_, G_ + 1):
                    ins = act.activation(x, y_, ACT.Silu)
                elif t in (CB_, CB_ + 1):
                    ins = act.activation(x, y_, ACT.Sigmoid)
                elif t in (SQ_, SQ_ + 1):
                    for c0, c1, r0, r1 in ((0, 4, 0, 64), (4, 5, 0, 32), (4, 5, 32, 64), (5, 9, 0, 64)):
                        t0 = CHUNK * c0 + r0
                        src = ps[:, 2 * (t % 2) + t0 // HT, t0 % HT:t0 % HT + (c1 - c0) * (r1 - r0)]
                        ins = act.activation(q_sw[:, c0:c1, t - SQ_, r0:r1], src.rearrange("p (c t) -> p c t", c=c1 - c0), ACT.Copy)
                else:
                    ins = act.activation(x, y_, ACT.Copy, scale=HD ** -0.5 if t in (BQ_, BQ_ + 1) else 1.0)
                ins.then_inc(proj_out, 1)
            next_proj[0] += n

        def tok_n(tb):
            return min(128, T - 128 * tb)

        def nblk(tb):
            return tok_n(tb) // LB

        def hg_turn(pe, tb):
            if tb == 0:
                pe.wait_ge(hg_kd, 2)
                pe.wait_ge(proj_out, V_ + 2)
            if tb >= 1:
                pe.wait_ge(hg_tok, tb)
            n, t0 = tok_n(tb), 128 * tb
            for q, x in enumerate((dsuf[:, 0, :], dsuf[:, 1, :], proj[:, V_, :], proj[:, V_ + 1, :])):
                ins = pe.transpose(ps[0:n, 4, 128 * q:128 * q + 128], x[:, t0:t0 + n], ident[:])
            ins.then_inc(hg_turned, 1)

        def hg_update(pe, tb, c):
            n = tok_n(tb)
            pe.wait_ge(hg_vm, 2 * tb + c + 1)
            if tb:
                pe.wait_ge(hg_state, tb)
            for a2 in range(2):
                ins = pe.matmul(ps[64 * a2:64 * a2 + 64, 6 + c, 0:HD * nblk(tb)], kvtok[0:n, tb % 2, 64 * (2 * c + a2):64 * (2 * c + a2) + 64],
                                vmask[c][0:n, a2, 0:nblk(tb), :].rearrange("p b v -> p (b v)"), start=True, stop=True)
            ins.then_inc(hg_upd, 1)

        def hg_states_out(pe, tb):
            pe.wait_ge(hg_state, tb + 1)
            if tb:
                pe.wait_ge(hg_inter_in, tb)
            for b in range(nblk(tb)):
                for c in range(2):
                    for a2 in range(2):
                        hh = slice(64 * a2, 64 * a2 + 64)
                        t0 = 128 * tb + LB * b
                        ins = pe.matmul(ps[hh, 5, 128 * c + LB * b:128 * c + LB * b + LB], states[hh, tb % 2, c, b, :],
                                        gpre[hh, c, t0:t0 + LB], start=True, stop=True)
            ins.then_inc(hg_inter, 1)

        def blocks(ap):
            return ap.rearrange("p (b t) -> p b t", t=LB)

        def hg_distance(pe, s_):
            d, c = divmod(s_, 2)
            n = NBLK // 2 * (LB - d)
            pe.wait_ge(hg_w, s_ + 1)
            if s_ >= 2:
                pe.wait_ge(hg_acc, s_ - 1)
            if s_ < 2:
                pe.wait_ge(hg_inter_in, TB)
            for f in range(2):
                ins = pe.matmul(ps[:, 4 + 2 * c + f, 0:n], headones[:], sq[:, c, n * f:n * f + n], start=True, stop=True)
            ins.then_inc(hg_att, 1)

        def hg_norm_pe(pe, c):
            pe.wait_ge(hg_sq, c + 1)
            ones_product(pe, 2 + c, headones[:], sq[:, c, :]).then_inc(hg_ss, 1)

        def act_hg(act):
            for tb in range(TB):
                n = tok_n(tb)
                act.wait_ge(hg_turned, tb + 1)
                if tb >= 2:
                    act.wait_ge(hg_upd, 2 * (tb - 1))
                    act.wait_ge(hg_vm, 2 * (tb - 1))
                act.activation(kvtok[0:n, tb % 2, :], ps[0:n, 4, :], ACT.Copy).then_inc(hg_tok, 1)
                act_proj_some(act, 1)

        def act_hg_out(act, L):
            act.wait_ge(hg_state, TB)
            for name, tile, last in (("hgrn_prompt", TB - 2, 8), ("hgrn_sample", TB - 1, 4)):
                act.dma_start(o[name][bass.ds(L, 1), 0].rearrange("l (c a) k v -> (a k) (l c) v", a=2), states[:, tile % 2, :, last, :]).then_inc(outs, 16)

        def act_hg_norm(act):
            act.preload_act_table_set(ROOT_SET)
            for c in range(2):
                act.wait_ge(hg_o, c + 1)
                act.activation(sq[:, c, :], of[:, 2 + c, :], ACT.Square).then_inc(hg_sq, 1)
            for c in range(2):
                act.wait_ge(hg_ss, c + 1)
                act.activation(halves((std, sqsum)[c][:]), pair(2 + c), ACT.Sqrt, bias=eps_col[:], scale=1.0 / HD).then_inc(hg_std, 1)
            act_proj_some(act, 1)

        def dve_hg(dve):
            lk = lambda ins: link(dve, ins)
            lk(dve.tensor_scalar(lb1m[:], lb[:], -1.0, 1.0, ALU.mult, ALU.add))
            for c in range(2):
                f, k = proj[:, F_ + c, :], kgate[:, c, :]
                dve.wait_ge(proj_out, F_ + c + 1)
                lk(dve.tensor_scalar(f, f, lb1m[:, c:c + 1], lb[:, c:c + 1], ALU.mult, ALU.add))
                lk(dve.tensor_scalar(k, k, lb1m[:, c:c + 1], None, ALU.mult))
                lk(dve.memset(dsuf[:, c, :], 0.0))
                lk(dve.tensor_copy(blocks(dsuf[:, c, :])[:, :, 0:1], blocks(f)[:, :, 0:1]))
                lk(dve.memset(blocks(f)[:, :, 0:1], 0.0))
                lk(dve.tensor_tensor_scan(gpre[:, c, :], f, dsuf[:, c, :], 0.0, ALU.mult, ALU.add))
                lk(dve.memset(dsuf[:, c, T - 1:T], 1.0))
                lk(dve.tensor_tensor_scan(dsuf[:, c, 0:T - 1][:, ::-1], f[:, 1:T][:, ::-1], blockend[:, 0:T - 1][:, ::-1],
                                          1.0, ALU.mult, ALU.add))
                lk(dve.tensor_copy(glast[:, c, :].unsqueeze(2), blocks(gpre[:, c, :])[:, :, LB - 1:LB]))
                dve.wait_ge(proj_out, Q_ + c + 1)
                lk(dve.tensor_tensor(gpre[:, c, :], gpre[:, c, :], proj[:, Q_ + c, :], ALU.mult))
                dve.tensor_tensor(dsuf[:, c, :], dsuf[:, c, :], k, ALU.mult).then_inc(hg_kd, 1)
            def mask_values(tb):
                n, nb = tok_n(tb), nblk(tb)
                dve.wait_ge(hg_tok, tb + 1)
                for c in range(2):
                    for a2 in range(2):
                        v = kvtok[0:n, tb % 2, 256 + 64 * (2 * c + a2):256 + 64 * (2 * c + a2) + 64]
                        ins = dve.tensor_tensor(vmask[c][0:n, a2, 0:nb, :], v.unsqueeze(1).to_broadcast([n, nb, HD]),
                                                blockmask[0:n, 0:nb].unsqueeze(2).to_broadcast([n, nb, HD]), ALU.mult)
                    ins.then_inc(hg_vm, 1)

            mask_values(0)
            for tb in range(TB):
                n, nb = tok_n(tb), nblk(tb)
                if tb >= 2:
                    dve.wait_ge(hg_inter, tb - 1)
                first = states[:, tb % 2, :, 0, :]
                if tb == 0:
                    lk(dve.memset(first, 0.0))
                elif tb == TB - 1:
                    dve.wait_ge(cache_in, CACHE_HG)
                    lk(dve.tensor_copy(first, hgs0[:]))
                else:
                    lk(dve.tensor_copy(first, states[:, (tb - 1) % 2, :, 8, :]))
                dve.wait_ge(hg_upd, 2 * tb + 2)
                for b in range(nb):
                    if b:
                        dve.wait_ge(dve_step, steps[0] - 1)
                    for c in range(2):
                        ins = dve.scalar_tensor_tensor(out=states[:, tb % 2, c, b + 1, :], in0=states[:, tb % 2, c, b, :],
                                                       scalar=glast[:, c, 8 * tb + b:8 * tb + b + 1], in1=ps[:, 6 + c, HD * b:HD * b + HD],
                                                       op0=ALU.mult, op1=ALU.add)
                        if b == nb - 1 and c == 1:
                            ins.then_inc(hg_state, 1)
                        else:
                            ins.then_inc(dve_step, 1)
                            steps[0] += 1
                            if c == 0 and b:
                                dve.wait_ge(dve_step, steps[0] - 1)
                dve.wait_ge(dve_step, steps[0])
                dve.wait_ge(hg_state, tb + 1)
                if tb + 1 < TB:
                    mask_values(tb + 1)
                dve.wait_ge(hg_inter, tb + 1)
                dve.tensor_copy(of[:, 2:4, 128 * tb:128 * tb + n], ps[:, 5, 0:256].rearrange("p (c t) -> p c t", c=2)[:, :, 0:n]).then_inc(hg_inter_in, 1)
            dve.wait_ge(hg_inter_in, TB)

            def take(s_):
                d, c = divmod(s_, 2)
                dve.wait_ge(hg_att, s_ + 1)
                att = ps[:, 4 + 2 * c:6 + 2 * c, 0:NBLK // 2 * (LB - d)].rearrange("p f (b t) -> p f b t", t=LB - d)
                v = proj[:, V_ + c, :].rearrange("p (f b t) -> p f b t", f=2, t=LB)[:, :, :, 0:LB - d]
                pr = rstd[:, 0:NBLK * (LB - d)]
                ins = dve.tensor_tensor(pr.rearrange("p (f b t) -> p f b t", f=2, t=LB - d), att, v, ALU.mult)
                ins.then_inc(hg_acc, 1)
                dve.wait_ge(hg_acc, s_ + 1)
                ov = blocks(of[:, 2 + c, :])[:, :, d:LB]
                ins = dve.tensor_tensor(ov, ov, pr.rearrange("p (b t) -> p b t", t=LB - d), ALU.add)
                if d == LB - 1:
                    ins.then_inc(hg_o, 1)
                    dve.wait_ge(hg_o, c + 1)
                else:
                    lk(ins)

            for s_ in range(2 * LB):
                d, c = divmod(s_, 2)
                w = sq[:, c, 0:NBLK * (LB - d)].rearrange("p (b t) -> p b t", t=LB - d)
                q = blocks(proj[:, Q_ + c, :])[:, :, d:LB]
                if d:
                    lk(dve.tensor_tensor(q, q, blocks(proj[:, F_ + c, :])[:, :, 1:LB + 1 - d], ALU.mult))
                if s_ >= 2:
                    dve.wait_ge(hg_att, s_ - 1)
                dve.tensor_tensor(w, q, blocks(kgate[:, c, :])[:, :, 0:LB - d], ALU.mult).then_inc(hg_w, 1)
                if s_:
                    take(s_ - 1)
            take(2 * LB - 1)
            for c in range(2):
                dve.wait_ge(hg_std, c + 1)
                lk(dve.reciprocal(rstd[:], (std, sqsum)[c][:]))
                x = of[:, 2 + c, :]
                lk(dve.scalar_tensor_tensor(out=x, in0=x, scalar=hgn[:], in1=rstd[:], op0=ALU.mult, op1=ALU.mult))
                dve.tensor_tensor(x, x, proj[:, G_ + c, :], ALU.mult).then_inc(hg_done, 1)
            dve.wait_ge(hg_done, 2)

        def pe_conv(pe):
            pe.wait_ge(cache_in, CACHE_SHORT)
            pe.wait_ge(hg_std, 2)
            for c in range(2):
                ins = pe.transpose(ps[:, 4, HIST * c:HIST * c + HIST], chist[0:HIST, 128 * c:128 * c + 128], ident[0:HIST, 0:HIST])
            ins.then_inc(cv_hist, 1)
            pe.wait_ge(cv_z, 2)
            for q, (c, t0) in enumerate(((0, SEQ), (1, SEQ), (0, ZW - HIST), (1, ZW - HIST))):
                ins = pe.transpose(ps[0:HIST, 6, 128 * q:128 * q + 128], zc[:, c, t0:t0 + HIST], ident[:])
            ins.then_inc(cv_tail, 1)
            for t in range(PROJ_CONV + 1, NPROJ):
                pe_proj(pe, t)
            for g in range(GATES_CONV - 2):
                pe_kept_gate(pe, g)
            pe.wait_ge(cv_y, 2)
            for t0, t1, y0 in ((0, SEQ, 0), (SEQ, T, SEQ + HIST)):
                for c in range(2):
                    ins = pe.matmul(flat(2)[:, t0:t1], ones[:], yc[:, c, y0:y0 + t1 - t0], start=c == 0, stop=c == 1)
            ins.then_inc(cv_mean, 1)
            pe_kept_gate(pe, GATES_CONV - 2)
            pe.wait_ge(cv_sq, 2)
            pe.wait_ge(cv_out, 1)
            for t0, t1 in ((0, SEQ), (SEQ, T)):
                for c in range(2):
                    ins = pe.matmul(flat(3)[:, t0:t1], ones[:], sq[:, c, t0:t1], start=c == 0, stop=c == 1)
            ins.then_inc(cv_var, 1)
            pe_kept_gate(pe, GATES_CONV - 1)

        PROJ_CONV = BK_ + 1
        GATES_CONV, GATES_SW = 8, 11
        SIG_LATER = GATES_CONV - 2

        def pe_gate_free(pe, g):
            split_ready(pe, U0_GATE + g)
            if g == 0:
                pe.wait_ge(proj_out, NPROJ)
            elif g < GATES_CONV:
                pe.wait_ge(gate_out, g - 1)
            else:
                pe.wait_ge(gate_out, g)

        def pe_kept_gate(pe, g):
            pe_gate_free(pe, g)
            products(pe, (U0_GATE + g) % SPLIT, u_hi, u_lo, range(KD), 0, g % 2, True, True).then_inc(unit_done, 1)

        def pe_gate_part(pe, n, last, step, parts):
            g, j = n + step // len(parts), step % len(parts)
            if g < last:
                if j == 0:
                    pe_gate_free(pe, g)
                unit_part(pe, U0_GATE + g, j, 0, parts)

        def act_gate_part(act, n, last, step, parts):
            g, j = n + step // len(parts), step % len(parts)
            if g < last and j == len(parts) - 1:
                act.wait_ge(unit_done, done(U0_GATE + g))
                if g == CA_:
                    act.wait_ge(cv_z, 2)
                if g == SQ_:
                    act.wait_ge(sw_score, len(SW))
                act.activation(halves(gkeep[:, g, :]), pair(0), ACT.Copy).then_inc(gate_out, 1)

        def act_kept_gate(act, g):
            act.wait_ge(unit_done, done(U0_GATE + g))
            if g == 0:
                act.wait_ge(hg_done, 2)
            act.activation(halves(gkeep[:, g, :]), pair(g % 2), ACT.Copy if g >= SIG_LATER else ACT.Sigmoid).then_inc(gate_out, 1)

        def act_conv(act, L):
            act.wait_ge(cv_tail, 1)
            act.activation(ctail[0:HIST].rearrange("p q c -> p (q c)"), ps[0:HIST, 6, :], ACT.Copy).then_inc(cv_out, 1)
            act.wait_ge(cv_out, 1)
            act.dma_start(o["conv_prompt"][bass.ds(L, 1), 0].rearrange("l t (q c) -> t (l q) c", q=2), ctail[0:HIST, 0:2, :]).then_inc(outs, 16)
            act.dma_start(o["conv_sample"][bass.ds(L, 1), 0].rearrange("l t (q c) -> t (l q) c", q=2), ctail[0:HIST, 2:4, :]).then_inc(outs, 16)
            act_proj_some(act, NPROJ - PROJ_CONV - 1)
            for g in range(SIG_LATER):
                act_kept_gate(act, g)
            act.preload_act_table_set(ROOT_SET)
            for c in range(2):
                act.wait_ge(cv_xc, c + 1)
                act.activation(sq[:, c, :], xc[:, c, :], ACT.Square).then_inc(cv_sq, 1)
            act_kept_gate(act, SIG_LATER)
            act.wait_ge(cv_var, 1)
            act.activation(std[:], flat(3), ACT.Sqrt, bias=eps_col[:], scale=1.0 / 256).then_inc(cv_std, 1)
            for c in range(2):
                act.wait_ge(cv_norm, c + 1)
                act.activation(of[:, c, :], xc[:, c, :], ACT.Silu, bias=crow[:, R_LNB, c:c + 1]).then_inc(cv_out, 1)
            act.preload_act_table_set(EXP_LN_SET)
            act_kept_gate(act, SIG_LATER + 1)

        def dve_conv(dve):
            lk = lambda ins: link(dve, ins)
            lk(dve.memset(zc[:, :, 0:HIST], 0.0))
            dve.wait_ge(cv_hist, 1)
            lk(dve.tensor_copy(zc[:, :, HIST + SEQ:HIST + SEQ + HIST], ps[:, 4, 0:2 * HIST].rearrange("p (c t) -> p c t", c=2)))
            for c in range(2):
                dve.wait_ge(proj_out, CB_ + c + 1)
                ca, cb = proj[:, CA_ + c, :], proj[:, CB_ + c, :]
                lk(dve.tensor_tensor(zc[:, c, HIST:HIST + SEQ], ca[:, 0:SEQ], cb[:, 0:SEQ], ALU.mult))
                dve.tensor_tensor(zc[:, c, ZW - DEC:ZW], ca[:, SEQ:T], cb[:, SEQ:T], ALU.mult).then_inc(cv_z, 1)
            dve.wait_ge(cv_z, 2)
            for w in range(CW):
                for c in range(2):
                    wc = taps[:, w, c:c + 1]
                    if w == 0:
                        ins = dve.tensor_scalar(yc[:, c, :], zc[:, c, 0:YW], wc, crow[:, R_CONVB, c:c + 1], ALU.mult, ALU.add)
                    else:
                        ins = dve.scalar_tensor_tensor(out=yc[:, c, :], in0=zc[:, c, w:w + YW], scalar=wc, in1=yc[:, c, :], op0=ALU.mult, op1=ALU.add)
                    if w < CW - 1:
                        lk(ins)
                    else:
                        ins.then_inc(cv_y, 1)
            dve.wait_ge(cv_mean, 1)
            dve.wait_ge(cv_y, 2)
            for c in range(2):
                lk(dve.scalar_tensor_tensor(out=xc[:, c, SEQ:T], in0=flat(2)[:, SEQ:T], scalar=-1.0 / 256, in1=yc[:, c, SEQ + HIST:YW], op0=ALU.mult, op1=ALU.add))
                dve.scalar_tensor_tensor(out=xc[:, c, 0:SEQ], in0=flat(2)[:, 0:SEQ], scalar=-1.0 / 256, in1=yc[:, c, 0:SEQ],
                                         op0=ALU.mult, op1=ALU.add).then_inc(cv_xc, 1)
            dve.wait_ge(cv_std, 1)
            lk(dve.reciprocal(rstd[:], std[:]))
            dve.wait_ge(cv_xc, 2)
            dve.wait_ge(cv_sq, 2)
            for c in range(2):
                dve.scalar_tensor_tensor(out=xc[:, c, :], in0=xc[:, c, :], scalar=crow[:, R_LNG, c:c + 1], in1=rstd[:],
                                         op0=ALU.mult, op1=ALU.mult).then_inc(cv_norm, 1)

        SW = list(range(SEQ // CHUNK + 1))

        def sw_blocks(ch):
            if ch == SEQ // CHUNK:
                return [(0, 9), (1, 10), (2, ch)]
            return [(j, ch - 2 + j) for j in range(3) if ch - 2 + j >= 0]

        def pe_sw_tok(pe):
            pe.wait_ge(cv_std, 1)
            pe.transpose(ps[:, 4, 0:128], swk_c[:], ident[:])
            for b in range(9):
                pe.transpose(ps[0:64, 5 + b // 4, 128 * (b % 4):128 * (b % 4) + 128], proj[:, SV_, 64 * b:64 * b + 64], ident[:])
            pe.transpose(ps[:, 7, 128:256], proj[:, SK_, SEQ - WINDOW:SEQ], ident[:])
            pe.transpose(ps[0:64, 7, 256:384], proj[:, SK_, SEQ:T], ident[:]).then_inc(sw_turn, 1)

        def sw_scores(pe, i):
            if i == 0:
                pe.wait_ge(sw_tok, 6)
            if i:
                pe.wait_ge(sw_scaled, i)
            for v in range(2):
                hv = slice(64 * v, 64 * v + 64)
                q = q_sw[hv, i, :, :].rearrange("p g t -> p (g t)")
                if i == SEQ // CHUNK:
                    pe.matmul(ps[:, 4 + v, 0:128], q, swkT_c[hv, :], start=True, stop=True)
                    ins = pe.matmul(ps[:, 4 + v, 128:192], q, proj[hv, SK_, SEQ:T], start=True, stop=True)
                else:
                    t0 = max(0, 64 * i - WINDOW)
                    ins = pe.matmul(ps[:, 4 + v, 192 - (64 * i + 64 - t0):192], q, proj[hv, SK_, t0:64 * i + 64], start=True, stop=True)
            ins.then_inc(sw_score, 1)

        def sw_turn_p(pe, i):
            pe.wait_ge(sw_prob, i + 1)
            if i:
                pe.wait_ge(sw_pTs, i)
            for v in range(2):
                for j, _ in sw_blocks(i):
                    ins = pe.transpose(ps[0:64, 6 + v, 128 * j:128 * j + 128], sc[:, i % 2, v, 64 * j:64 * j + 64], ident[:])
            ins.then_inc(sw_pT, 1)

        def sw_values(pe, i):
            pe.wait_ge(sw_pTs, i + 1)
            if i >= 2:
                pe.wait_ge(sw_o, i - 1)
            bl = sw_blocks(i)
            for v in range(2):
                for n, (j, b) in enumerate(bl):
                    ins = pe.matmul(ps[64 * v:64 * v + 64, 2 + i % 2, 0:128], v64[0:64, b, 64 * v:64 * v + 64], pT[0:64, i % 2, v, j, :],
                                    start=n == 0, stop=n == len(bl) - 1)
            ins.then_inc(sw_pv, 1)

        def pe_sw(pe):
            for i in range(len(SW) + 2):
                if i < len(SW):
                    sw_scores(pe, i)
                pe_gate_part(pe, GATES_CONV, GATES_SW, i, THIRDS)
                if 0 <= i - 1 < len(SW):
                    sw_turn_p(pe, i - 1)
                if 0 <= i - 2:
                    sw_values(pe, i - 2)

        def act_sw(act, L):
            act.wait_ge(sw_turn, 1)
            act.activation(swkT_c[:], ps[:, 4, 0:128], ACT.Copy).then_inc(sw_tok, 1)
            act.activation(v64[0:64, 0:4, :].rearrange("p b c -> p (b c)"), ps[0:64, 5, :], ACT.Copy).then_inc(sw_tok, 1)
            act.activation(v64[0:64, 4:8, :].rearrange("p b c -> p (b c)"), ps[0:64, 6, :], ACT.Copy).then_inc(sw_tok, 1)
            act.activation(v64[0:64, 8, :], ps[0:64, 7, 0:128], ACT.Copy).then_inc(sw_tok, 1)
            act.activation(swk_tok[:, 0, :], ps[:, 7, 128:256], ACT.Copy).then_inc(sw_tok, 1)
            act.activation(v64[0:64, 9:11, :], swv_c[0:64], ACT.Copy)
            act.activation(swk_tok[0:64, 1, :], ps[0:64, 7, 256:384], ACT.Copy).then_inc(sw_tok, 1)
            act.wait_ge(sw_tok, 6)

            def out(name, t0, n, src):
                x = o[name][bass.ds(L, 1), 0, t0:t0 + n].rearrange("l t h d -> (l t) (h d)")
                if len(src.shape) == 3:
                    x = x.rearrange("(b p) c -> p b c", p=64)
                act.dma_start(x, src).then_inc(outs, 16)

            out("swa_k_prompt", 0, 128, swk_tok[:, 0, :])
            out("swa_v_prompt", 0, 128, v64[0:64, 6:8, :])
            out("swa_k_sample", 0, 64, swk_c[64:128, :])
            out("swa_k_sample", 64, 64, swk_tok[0:64, 1, :])
            out("swa_v_sample", 0, 64, swv_c[0:64, 1, :])
            out("swa_v_sample", 64, 64, v64[0:64, 8, :])

            for i in range(len(SW) + 2):
                if i < len(SW):
                    k0 = 64 * sw_blocks(i)[0][0]
                    st = stat[:, i % 2]
                    act.wait_ge(sw_max, i + 1)
                    for v in range(2):
                        x = sc[:, i % 2, v, k0:192]
                        act.activation(x, x, ACT.Exp, bias=st[:, 1, v:v + 1], accum_out=st[:, 3, v:v + 1])
                    act.activation(st[:, 4, :], st[:, 2, :], ACT.Exp).then_inc(sw_exp, 1)
                if 1 <= i <= len(SW):
                    j0 = sw_blocks(i - 1)[0][0]
                    act.wait_ge(sw_pT, i)
                    if i >= 3:
                        act.wait_ge(sw_pv, i - 2)
                    act.activation(pT[0:64, (i - 1) % 2, :, j0:3, :].rearrange("p v j q -> p v (j q)"), ps[0:64, 6:8, 128 * j0:384], ACT.Copy).then_inc(sw_pTs, 1)
                if i >= 2:
                    act.wait_ge(sw_pv, i - 1)
                    act.activation(of[:, 4:6, 64 * (i - 2):64 * (i - 2) + 64], ps[:, 2 + i % 2, 0:128].rearrange("p (g q) -> p g q", g=2), ACT.Copy).then_inc(sw_o, 1)
                act_gate_part(act, GATES_CONV, GATES_SW, i, THIRDS)

        def dve_sw(dve):
            lk = lambda ins: link(dve, ins)

            def prob(i):
                k0 = 64 * sw_blocks(i)[0][0]
                x, st = sc[:, i % 2, :, k0:192], stat[:, i % 2]
                dve.wait_ge(sw_exp, i + 1)
                lk(dve.tensor_tensor(st[:, 5, :], st[:, 3, :], st[:, 4, :], ALU.add))
                lk(dve.reciprocal(st[:, 5, :], st[:, 5, :]))
                dve.tensor_tensor(x, x, st[:, 5, :].unsqueeze(2).to_broadcast([128, 2, 192 - k0]), ALU.mult).then_inc(sw_prob, 1)

            for i in SW:
                k0 = 64 * sw_blocks(i)[0][0]
                x, st = sc[:, i % 2, :, k0:192], stat[:, i % 2]
                if i:
                    prob(i - 1)
                if i >= 2:
                    dve.wait_ge(sw_pT, i - 1)
                dve.wait_ge(sw_score, i + 1)
                dve.scalar_tensor_tensor(out=x, in0=ps[:, 4:6, k0:192], scalar=HD ** -0.5, in1=alibi[:, :, k0:192], op0=ALU.mult, op1=ALU.add).then_inc(sw_scaled, 1)
                dve.wait_ge(sw_scaled, i + 1)
                lk(dve.tensor_reduce(st[:, 0, :], x, AX.X, ALU.max))
                lk(dve.tensor_tensor(st[:, 0, :], st[:, 0, :], sinkcol[:], ALU.max))
                lk(dve.tensor_scalar(st[:, 1, :], st[:, 0, :], -1.0, None, ALU.mult))
                dve.tensor_tensor(st[:, 2, :], sinkcol[:], st[:, 1, :], ALU.add).then_inc(sw_max, 1)
            prob(len(SW) - 1)

        SB = [(hd, kb) for hd in range(4) for kb in (3, 2, 1, 0)] + [(None, kb) for kb in (None, 3, 2, 1, 0)]

        def sb_shape(i):
            hd, kb = SB[i]
            if hd is None:
                return (64 if kb is None else 128), 4 * DEC
            return 128, SEQ - 128 * kb

        def sb_first(i):
            return i == 0 or SB[i][0] != SB[i - 1][0]

        def sb_diagonal(i):
            hd, kb = SB[i]
            return hd is not None or kb is None

        def sb_sums(i):
            return sum(SB[j][1] != 0 for j in range(i + 1))

        def pe_sb_tok(pe):
            pe.wait_ge(sw_o, len(SW))
            pe.wait_ge(cache_in, CACHE_SB)
            for tb in range(TB):
                if tb >= 2:
                    pe.wait_ge(sb_tok, tb - 1)
                for q, x in enumerate((BK_, BK_ + 1, BV_, BV_ + 1)):
                    n = tok_n(tb)
                    ins = pe.transpose(ps[0:n, 4 + tb % 2, 128 * q:128 * q + 128], proj[:, x, 128 * tb:128 * tb + n], ident[:])
                ins.then_inc(sb_turn, 1)
            for c in range(2):
                for kb in range(4):
                    ins = pe.transpose(ps[:, 6 + c, 128 * kb:128 * kb + 128], sbk_c[:, kb, 128 * c:128 * c + 128], ident[:])
                ins.then_inc(sb_turn, 1)

        def sb_logits(pe, i):
            hd, kb = SB[i]
            bk = 4 + i % 2
            if i == 0:
                pe.wait_ge(sb_tok, TB + 2)
            if i >= 2:
                pe.wait_ge(sb_min, i - 1)
            if hd is not None:
                hh, c = slice(64 * (hd % 2), 64 * (hd % 2) + 64), hd // 2
                pe.matmul(ps[:, bk, 0:SEQ - 128 * kb], proj[hh, BK_ + c, 128 * kb:128 * kb + 128], proj[hh, BQ_ + c, 128 * kb:SEQ],
                          start=True, stop=True).then_inc(sb_z, 1)
                return
            for q in (0, 2, 1, 3):
                hh, c = slice(64 * (q % 2), 64 * (q % 2) + 64), q // 2
                if q == 1:
                    pe.wait_ge(sb_zrow, i - 4 * 4 + 1)
                k = proj[hh, BK_ + c, SEQ:T] if kb is None else sbkT_c[hh, c, 128 * kb:128 * kb + 128]
                ins = pe.matmul(ps[0:sb_shape(i)[0], bk, 64 * q:64 * q + 64], k, proj[hh, BQ_ + c, SEQ:T],
                                start=q == 0, stop=q == 3, skip_group_check=True)
                if q == 2:
                    ins.then_inc(sb_zrow, 1)
            ins.then_inc(sb_z, 1)

        def sb_rest(pe, i):
            nk, w = sb_shape(i)
            bk = 4 + i % 2
            pe.wait_ge(sb_sp, i + 1)
            ins = pe.matmul(ps[0:nk, bk, 0:w], trineg[0:nk, 0:nk], spx[0:nk, i % 2, 0:w], start=False, stop=sb_first(i), skip_group_check=True)
            if not sb_first(i):
                q0, z0 = (0, 0) if SB[i][0] is None else (128 * SB[i][1] + 128, 128)
                pe.wait_ge(sb_sum, sb_sums(i - 1))
                ins = pe.matmul(ps[:, bk, z0:w], negones[:], sqsum[:, q0:q0 + w - z0], start=False, stop=True, skip_group_check=True)
            ins.then_inc(sb_arg, 1)

        def sb_values(pe, i):
            hd, kb = SB[i]
            nk, w = sb_shape(i)
            if sb_diagonal(i):
                pe.wait_ge(sb_a, sum(sb_diagonal(j) for j in range(i + 1)))
            else:
                pe.wait_ge(sb_exp, i + 1)
            if hd is not None:
                if sb_first(i) and hd >= 2:
                    pe.wait_ge(sb_o, hd - 1)
                hh = slice(64 * (hd % 2), 64 * (hd % 2) + 64)
                pe.matmul(ps[hh, 6 + hd % 2, 128 * kb:SEQ], sbtok[:, kb, 256 + 64 * hd:256 + 64 * hd + 64], arg[:, i % 2, 0:w],
                          start=sb_first(i), stop=kb == 0, skip_group_check=True).then_inc(sb_pv, 1)
                return
            for q in range(4):
                hh, c = slice(64 * (q % 2), 64 * (q % 2) + 64), q // 2
                v = sbtok[0:64, TB - 1, 256 + 64 * q:256 + 64 * q + 64] if kb is None else sbv_c[:, kb, 64 * q:64 * q + 64]
                ins = pe.matmul(ps[hh, 2, 64 * c:64 * c + 64], v, arg[0:nk, i % 2, 64 * q:64 * q + 64],
                                start=sb_first(i) and c == 0, stop=kb == 0, skip_group_check=True)
            ins.then_inc(sb_pv, 1)

        def pe_sb(pe):
            for i in range(len(SB) + 2):
                if i < len(SB):
                    sb_logits(pe, i)
                if 0 <= i - 1 < len(SB):
                    sb_rest(pe, i - 1)
                if i >= 2:
                    sb_values(pe, i - 2)
                pe_gate_part(pe, GATES_SW, 2 * KD, i, QUARTERS)

        def act_sb(act, L):
            def out(name, t0, n, src):
                x = o[name][bass.ds(L, 1), 0, t0:t0 + n].rearrange("l t h d -> (l t) (h d)")
                if len(src.shape) == 3:
                    x = x.rearrange("(b p) c -> p b c", p=128)
                act.dma_start(x, src).then_inc(outs, 16)

            for tb in range(TB):
                act.wait_ge(sb_turn, tb + 1)
                act.activation(sbtok[0:tok_n(tb), tb, :], ps[0:tok_n(tb), 4 + tb % 2, :], ACT.Copy).then_inc(sb_tok, 1)
            for c in range(2):
                act.wait_ge(sb_turn, TB + c + 1)
                act.activation(sbkT_c[:, c, :], ps[:, 6 + c, :], ACT.Copy).then_inc(sb_tok, 1)
            act.wait_ge(sb_tok, TB)
            out("sb_k_prompt", 0, SEQ, sbtok[:, 0:4, 0:256])
            out("sb_v_prompt", 0, SEQ, sbtok[:, 0:4, 256:512])
            out("sb_k_sample", 0, DEC, sbtok[0:64, 4, 0:256])
            out("sb_v_sample", 0, DEC, sbtok[0:64, 4, 256:512])

            def evac(i):
                hd, kb = SB[i]
                if kb == 0:
                    act.wait_ge(sb_pv, i + 1)
                    if hd is None:
                        act.activation(of[:, 6:8, SEQ:T], ps[:, 2, 0:128].rearrange("p (c q) -> p c q", c=2), ACT.Copy).then_inc(sb_o, 1)
                    else:
                        hh = slice(64 * (hd % 2), 64 * (hd % 2) + 64)
                        act.activation(of[hh, 6 + hd // 2, 0:SEQ], ps[hh, 6 + hd % 2, :], ACT.Copy).then_inc(sb_o, 1)

            for i in range(len(SB) + 2):
                if i < len(SB):
                    nk, w = sb_shape(i)
                    x = sq[0:nk, i % 2, 0:w]
                    act.wait_ge(sb_z, i + 1)
                    if i >= 2:
                        act.wait_ge(sb_sp, i - 1)
                    act_link(act, act.activation(x, ps[0:nk, 4 + i % 2, 0:w], ACT.Abs))
                    act_link(act, act.activation(x, x, ACT.Exp, scale=-1.0))
                    act.activation(x, x, ACT.Ln, bias=ones[0:nk, 0:1]).then_inc(sb_ln, 1)
                if 0 <= i - 1 < len(SB):
                    nk, w = sb_shape(i - 1)
                    x = arg[0:nk, (i - 1) % 2, 0:w]
                    act.wait_ge(sb_min, i)
                    act.activation(x, x, ACT.Exp).then_inc(sb_exp, 1)
                if i >= 2:
                    evac(i - 2)
                act_gate_part(act, GATES_SW, 2 * KD, i, QUARTERS)

        def dve_sb(dve):
            lk = lambda ins: link(dve, ins)

            def mask(i, x):
                if SB[i][0] is None:
                    v = x[0:64, i % 2, 0:256].rearrange("p (h q) -> p h q", h=4)
                    return dve.tensor_tensor(v, v, later[0:64, 0:64].unsqueeze(1).to_broadcast([64, 4, 64]), ALU.mult)
                return dve.tensor_tensor(x[:, i % 2, 0:128], x[:, i % 2, 0:128], later[:], ALU.mult)

            def finish(i):
                hd, kb = SB[i]
                nk, w = sb_shape(i)
                dve.wait_ge(sb_arg, i + 1)
                if i >= 2:
                    dve.wait_ge(sb_pv, i - 1)
                dve.tensor_scalar(arg[0:nk, i % 2, 0:w], ps[0:nk, 4 + i % 2, 0:w], 0.0, None, ALU.min).then_inc(sb_min, 1)
                if kb != 0:
                    if hd is None:
                        if kb is None:
                            lk(dve.memset(sqsum[:, 0:w], 0.0))
                        ins = dve.tensor_tensor(sqsum[0:nk, 0:w], sqsum[0:nk, 0:w], spx[0:nk, i % 2, 0:w], ALU.add)
                    else:
                        q0 = 128 * kb
                        if not sb_first(i):
                            lk(dve.tensor_tensor(sqsum[:, q0 + 128:SEQ], sqsum[:, q0 + 128:SEQ], spx[:, i % 2, 128:w], ALU.add))
                        ins = dve.tensor_copy(sqsum[:, q0:q0 + 128], spx[:, i % 2, 0:128])
                    ins.then_inc(sb_sum, 1)
                    dve.wait_ge(sb_sum, sb_sums(i))
                if sb_diagonal(i):
                    dve.wait_ge(sb_exp, i + 1)
                    mask(i, arg).then_inc(sb_a, 1)

            for i in range(len(SB)):
                nk, w = sb_shape(i)
                z = ps[0:nk, 4 + i % 2, 0:w]
                if i:
                    finish(i - 1)
                dve.wait_ge(sb_ln, i + 1)
                ins = dve.scalar_tensor_tensor(out=spx[0:nk, i % 2, 0:w], in0=z, scalar=0.0, in1=sq[0:nk, i % 2, 0:w], op0=ALU.max, op1=ALU.add)
                if sb_diagonal(i):
                    lk(ins)
                    ins = mask(i, spx)
                ins.then_inc(sb_sp, 1)
            finish(len(SB) - 1)

        def pe_gates(pe):
            with pe.Fori(0, 2) as it:
                for m in range(4):
                    u0 = U0_PAIR + 3 * m
                    i = it * 12 + u0
                    split_ready(pe, i)
                    if m == 0:
                        pe.wait_ge(gate_out, 2 * KD)
                    for n in range(NB):
                        if m == 0:
                            pe.wait_ge(o_ready, 2 * n + 2)
                        if n >= 2:
                            pe.wait_ge(sig_done, it * 8 + (2 * m + n - 1))
                        ins = products(pe, u0 % SPLIT, o_hi, o_lo, (2 * n, 2 * n + 1), 2 * n, n, True, True)
                    ins.then_inc(unit_done, 1)
                    for n in (2, 3):
                        split_ready(pe, i + (n - 1))
                        pe.wait_ge(yb_out, it * 16 + (4 * m + n - 1))
                        products(pe, (u0 + n - 1) % SPLIT, u_hi, u_lo, range(KD), 0, n, True, True).then_inc(unit_done, 1)
                    pe.wait_ge(yb_out, it * 16 + (4 * m + 4))

        def pe_out(pe):
            for m in range(KD):
                i = U0_OUT + m
                split_ready(pe, i)
                if m >= 4:
                    pe.wait_ge(y_ready, y_before[N_MPOST] + m + 1)
                products(pe, i % SPLIT, m_split[:, :, 0, :], m_split[:, :, 1, :], range(KD), 0, m % 4, True, True,
                         wait_k=(lambda k: pe.wait_ge(m_ready, k + 1)) if m == 0 else None).then_inc(unit_done, 1)
            pe.wait_ge(y_ready, 4 + y_before[N_MPOST] + 5)
            pe_norm_y(pe, N_MPOST)

        def act_gates(act):
            for m in range(KD):
                u0 = U0_PAIR + 3 * m
                act.wait_ge(unit_done, done(u0))
                if m:
                    act.wait_ge(gated, 4 * m)
                for n in (2, 3, 0, 1):
                    act.activation(halves(ybr[:, n, :]), pair(n), ACT.Copy).then_inc(yb_out, 1)
                for g in (2 * m, 2 * m + 1):
                    if g >= SIG_LATER:
                        act.wait_ge(gate_out, g + 1)
                        act.activation(gkeep[:, g, :], gkeep[:, g, :], ACT.Sigmoid).then_inc(gate_sig, 1)
                for n in (2, 3):
                    act.wait_ge(unit_done, done(u0 + n - 1))
                    act.activation(halves(sg[:, n - 2, :]), pair(n), ACT.Sigmoid).then_inc(sig_done, 1)

        def dve_gates(dve):
            for m in range(KD):
                for n in range(NB):
                    if n < 2:
                        dve.wait_ge(yb_out, 4 * m + n + 3)
                        if m == 0 and n == 0:
                            dve.wait_ge(gate_out, SIG_LATER)
                        if 2 * m + n >= SIG_LATER:
                            dve.wait_ge(gate_sig, 2 * m + n - SIG_LATER + 1)
                    else:
                        dve.wait_ge(sig_done, 2 * m + n + 1)
                    gate = gkeep[:, 2 * m + n, :] if n < 2 else sg[:, n - 2, :]
                    dst = mprod[:, n % 2, :] if n else msum[:]
                    if m and n == 0:
                        dve.wait_ge(m_ready, m)
                    dve.tensor_tensor(dst, gate, ybr[:, n, :], ALU.mult).then_inc(gated, 1)
                    if n:
                        dve.wait_ge(gated, 4 * m + n + 1)
                        link(dve, dve.tensor_tensor(msum[:], msum[:], dst, ALU.add))
                link(dve, dve.tensor_copy(m_split[:, m, 0, :], msum[:]))
                dve.tensor_tensor(m_split[:, m, 1, :], msum[:], m_split[:, m, 0, :], ALU.subtract).then_inc(m_ready, 1)

        def pe_mixer(pe):
            pe_norm_h(pe, N_MPRE)
            for t in range(CA_):
                pe_proj(pe, t)
            hg_turn(pe, 0)
            for tb in range(TB):
                hg_update(pe, tb, 0)
                hg_update(pe, tb, 1)
                if tb + 1 < TB:
                    hg_turn(pe, tb + 1)
                pe_proj(pe, CA_ + tb)
                hg_states_out(pe, tb)
            for s_ in range(2 * LB):
                hg_distance(pe, s_)
                if s_ // 5 < PROJ_CONV - CA_ - TB:
                    pe_proj_part(pe, CA_ + TB + s_ // 5, s_ % 5, FIFTHS)
            for c in range(2):
                hg_norm_pe(pe, c)
            pe_proj(pe, PROJ_CONV)
            pe_conv(pe)
            pe_sw_tok(pe)
            pe_sw(pe)
            pe_sb_tok(pe)
            pe_sb(pe)
            pe_gates(pe)
            pe_out(pe)

        def act_mixer(act, L):
            act_norm_h(act, N_MPRE)
            act.wait_ge(u_ready, 2 * len(LO_DVE))
            act.wait_ge(u_ready_pool, 2 * len(LO_POOL))
            act.dma_start(hgs0[:], a["state_hgrn"][bass.ds(L, 1), 0].rearrange("l (c a) k v -> (a k) (l c) v", a=2)).then_inc(cache_in, 16)
            act.dma_start(chist[0:HIST, :], a["cache_conv"][bass.ds(L, 1), 0].rearrange("l t c -> (l t) c")).then_inc(cache_in, 16)
            act.dma_start(swk_c[:], a["cache_swa_k"][bass.ds(L, 1), 0].rearrange("l t h d -> (l t) (h d)")).then_inc(cache_in, 16)
            act.dma_start(swv_c[0:64], a["cache_swa_v"][bass.ds(L, 1), 0].rearrange("l (b p) h d -> p (l b) (h d)", p=64)).then_inc(cache_in, 16)
            act_proj_some(act, CA_)
            act_hg(act)
            act_proj_some(act, PROJ_CONV - CA_ - TB)
            act_hg_out(act, L)
            act_hg_norm(act)
            act.wait_ge(outs, 32)
            act.wait_ge(hg_inter, TB)
            act.dma_start(sbk_c[:], a["cache_sb_k"][bass.ds(L, 1), 0].rearrange("l (b p) h d -> p (l b) (h d)", p=128)).then_inc(cache_in, 16)
            act.dma_start(sbv_c[:], a["cache_sb_v"][bass.ds(L, 1), 0].rearrange("l (b p) h d -> p (l b) (h d)", p=128)).then_inc(cache_in, 16)
            act_conv(act, L)
            act.wait_ge(cv_out, 3)
            act_sw(act, L)
            act.wait_ge(outs, 64 + 96)
            act_sb(act, L)
            act.wait_ge(outs, 64 + 96 + 64)
            act.wait_ge(sb_o, 5)
            for t in range(2 * NB):
                act.activation(o_hi[:, t, :], of[:, t, :], ACT.Copy).then_inc(o_high, 1)
            act_gates(act)
            act.preload_act_table_set(ROOT_SET)
            for m in range(KD):
                act_y(act, N_MPOST, m, U0_OUT + m, m % 4)
            act_root(act, N_MPOST)

        def dve_mixer(dve, L):
            dve_apply(dve, N_MPRE)
            dve_hg(dve)
            dve.wait_ge(hg_std, 2)
            dve_conv(dve)
            dve.wait_ge(sw_tok, 6)
            dve_sw(dve)
            dve_sb(dve)
            for t in range(2 * NB):
                dve.wait_ge(o_high, t + 1)
                dve.tensor_tensor(o_lo[:, t, :], of[:, t, :], o_hi[:, t, :], ALU.subtract).then_inc(o_ready, 1)
            dve_gates(dve)
            for m in range(KD):
                dve_add_square(dve, N_MPOST, m)
            dve_residual(dve, N_MPOST, y)

        def pe_turn_p(pe):
            pe.wait_ge(tok_ple, 32)
            for c in range(2):
                pe.wait_ge(y_ready, 4 + y_before[N_F2POST] + 6 + c)
                for tb in range(TB):
                    n = tok_n(tb)
                    ins = pe.transpose(flat(1 + c)[:, 128 * tb:128 * tb + n], ptok[0:n, tb, 128 * c:128 * c + 128], ident[0:n, 0:n])
                ins.then_inc(p_turned, 1)

        def pe_ple(pe):
            for q in range(2):
                i = U0_PLEW + q
                split_ready(pe, i)
                pe.wait_ge(p_ready, 2)
                for m in range(4):
                    j = 4 * q + m
                    if j >= 3:
                        pe.wait_ge(e_out, j - 2)
                    for kk in range(2):
                        for c, (wt, x) in enumerate(((whi, p_hi), (whi, p_lo), (wlo, p_hi))):
                            for f in range(2):
                                ins = pe.matmul(ps[:, 2 * (j % 3) + f, 0:HT], wt[:, i % SPLIT, 512 * kk + 128 * m:512 * kk + 128 * m + 128],
                                                x[:, kk, HT * f:HT * f + HT], start=kk == 0 and c == 0, stop=kk == 1 and c == 2, skip_group_check=True)
                    ins.then_inc(e_made, 1)
                pe.wait_ge(e_made, 4 * q + 4)
                pe.sem_inc(unit_done, 1)
            pe.wait_ge(e_out, KD)
            pe_norm_h(pe, N_PPRE)
            for m in range(KD):
                i = U0_PLEG + m
                split_ready(pe, i)
                if m >= 4:
                    pe.wait_ge(ple_sig, m - 3)
                products(pe, i % SPLIT, u_hi, u_lo, range(KD), 0, m % 4, True, True,
                         wait_k=u_tile_ready(pe, N_PPRE) if m == 0 else None).then_inc(unit_done, 1)
            pe.wait_ge(ple_sig, 5)
            pe_norm_y(pe, N_PPOST)

        def act_turned_p(act):
            for c in range(2):
                act.wait_ge(p_turned, c + 1)
                act.activation(p_hi[:, c, :], flat(1 + c), ACT.Copy).then_inc(p_high, 1)

        def act_ple(act):
            def e_tile(m):
                act.wait_ge(e_made, m + 1)
                act.activation(halves(e[:, m, :]), pair(m % 3), ACT.Copy).then_inc(e_out, 1)

            for m in range(4):
                e_tile(m)
            act_square_h(act, N_PPRE, 0)
            act_square_h(act, N_PPRE, 1)
            for m in range(4, KD):
                e_tile(m)
            for k in range(2, KD):
                act_square_h(act, N_PPRE, k)
            act_norm_root(act, N_PPRE)
            for m in range(KD):
                act.wait_ge(unit_done, done(U0_PLEG + m))
                if m >= 2:
                    act.wait_ge(e_gated, m - 1)
                act.activation(halves(gsig[:, m % 2, :]), pair(m % 4), ACT.Sigmoid).then_inc(ple_sig, 1)
                if m == KD - 1:
                    act.preload_act_table_set(ROOT_SET)
                act.wait_ge(e_gated, m + 1)
                act_square(act, N_PPOST, m, e[:, m, :])
            act_root(act, N_PPOST)

        def dve_turned_p(dve):
            for c in range(2):
                dve.wait_ge(p_high, c + 1)
                dve.tensor_tensor(p_lo[:, c, :], flat(1 + c), p_hi[:, c, :], ALU.subtract).then_inc(p_ready, 1)

        def dve_ple(dve):
            dve_residual(dve, N_F2POST, y)
            dve_apply(dve, N_PPRE)
            for m in range(KD):
                dve.wait_ge(ple_sig, m + 1)
                dve.wait_ge(e_out, m + 1)
                dve.tensor_tensor(e[:, m, :], e[:, m, :], gsig[:, m % 2, :], ALU.mult).then_inc(e_gated, 1)
                if m:
                    dve_add_square(dve, N_PPOST, m - 1)
            dve_add_square(dve, N_PPOST, KD - 1)
            dve_residual(dve, N_PPOST, e)

        with nc.Fori(0, DEPTH) as L:
            with nc.Block() as block:

                @block.sync
                def _(sp_):
                    load_ffn(sp_, L, a["ffn1_up"], a["ffn1_down"], U0_FFN1)
                    for t in range(NPROJ):
                        i = U0_PROJ + t
                        slot = i % RAW
                        if t in (SQ_, SQ_ + 1):
                            for v in range(2):
                                c = C_SQ + 128 * v + 64 * (t - SQ_)
                                if v == 0:
                                    sp_.wait_ge(w_split, i + 1)
                                sp_.dma_start(wraw[:, slot, :].rearrange("p (k n) -> p k n", k=KD)[:, :, 64 * v:64 * v + 64],
                                              cols(a["w_in"], L, slice(c, c + 64))).then_inc(w_loaded[slot], 16)
                            continue
                        if t in (SK_, SV_):
                            c = C_SK if t == SK_ else C_SV
                        else:
                            g = max(x for x in PROJ_COL if x <= t)
                            c = PROJ_COL[g] + 128 * (t - g)
                        load_unit(sp_, slot, i, cols(a["w_in"], L, slice(c, c + 128)))
                    wb = a["w_branch"].rearrange("l n r c -> l (n r) c")
                    for g in range(2 * KD):
                        cg = C_GATE + D * (g % 2) + 128 * (g // 2)
                        load_unit(sp_, (U0_GATE + g) % RAW, U0_GATE + g, cols(a["w_in"], L, slice(cg, cg + 128)))
                    for m in range(KD):
                        i = U0_PAIR + 3 * m
                        slot, c = i % RAW, slice(128 * m, 128 * m + 128)
                        sp_.wait_ge(w_split, i + 1)
                        v = wraw[:, slot, :].rearrange("p (k n) -> p k n", k=8)
                        sp_.dma_start(v[:, 0:4, :], cols(wb, L, c, 0, 4)).then_inc(w_loaded[slot], 16)
                        for kv in range(2):
                            sp_.dma_start(v[64 * kv:64 * kv + 64, 4:6, :],
                                          wb[bass.ds(L, 1), 512 + 128 * kv:640 + 128 * kv, c].rearrange("l (g d) n -> d (l g) n", g=2)).then_inc(w_loaded[slot], 16)
                        sp_.dma_start(v[:, 6:8, :], cols(wb, L, c, 6, 2)).then_inc(w_loaded[slot], 16)
                        for n in (2, 3):
                            cg = C_GATE + D * n + 128 * m
                            load_unit(sp_, (i + n - 1) % RAW, i + n - 1, cols(a["w_in"], L, slice(cg, cg + 128)))
                    for m in range(KD):
                        i = U0_OUT + m
                        load_unit(sp_, i % RAW, i, cols(a["w_out"], L, slice(128 * m, 128 * m + 128)))
                    load_ffn(sp_, L, a["ffn2_up"], a["ffn2_down"], U0_FFN2)
                    for q in range(2):
                        i = U0_PLEW + q
                        sp_.wait_ge(w_split, i + 1)
                        sp_.dma_start(wraw[:, i % RAW, :].rearrange("p (k n) -> p k n", k=2),
                                      a["ple_w"][bass.ds(L, 1), :, 512 * q:512 * q + 512].rearrange("l (k p) n -> p (l k) n", p=128)).then_inc(w_loaded[i % RAW], 16)
                    for m in range(KD):
                        i = U0_PLEG + m
                        load_unit(sp_, i % RAW, i, cols(a["ple_gate_w"], L, slice(128 * m, 128 * m + 128)))

                @block.gpsimd
                def _(pool):
                    pool.sem_inc(w_split, RAW)
                    landed = [0] * RAW

                    def split(slot, i, i_part, n_landed):
                        pool.wait_ge(w_loaded[slot], n_landed)
                        pool.wait_ge(unit_done, i + 1)
                        pool.tensor_tensor(whi[:, i_part, :], wraw[:, slot, :], ones[:, 0:1].to_broadcast([128, 1024]), ALU.mult).then_inc(w_rounded, 1)
                        pool.wait_ge(w_rounded, i + 1)
                        pool.tensor_tensor(wlo[:, i_part, :], wraw[:, slot, :], whi[:, i_part, :], ALU.subtract).then_inc(w_split, 1)

                    def split_run(i0, i1):
                        assert (i1 - i0) % RAW == 0
                        with pool.Fori(0, (i1 - i0) // RAW) as it:
                            for q in range(RAW):
                                slot = (i0 + q) % RAW
                                split(slot, it * RAW + (i0 + q), (i0 + q) % SPLIT, it * 16 + (landed[slot] + 16))
                        for q in range(RAW):
                            landed[q] += 16 * (i1 - i0) // RAW

                    def split_one(i, dmas):
                        landed[i % RAW] += 16 * dmas
                        split(i % RAW, i, i % SPLIT, landed[i % RAW])

                    def straight(i0, i1):
                        for i in range(i0, i1):
                            branch = U0_PAIR <= i < U0_OUT and (i - U0_PAIR) % 3 == 0
                            swq = i - U0_PROJ in (SQ_, SQ_ + 1)
                            split_one(i, 4 if branch else 2 if swq else 1)

                    straight(0, 2)
                    pool_apply(pool, N_F1PRE)
                    straight(2, 4)
                    split_run(4, U0_PROJ)
                    straight(U0_PROJ, U0_PROJ + 2)
                    pool_residual(pool, N_F1POST)
                    pool_apply(pool, N_MPRE)
                    straight(U0_PROJ + 2, U0_FFN2 + 2)
                    pool_residual(pool, N_MPOST)
                    pool_apply(pool, N_F2PRE)
                    straight(U0_FFN2 + 2, U0_FFN2 + 4)
                    split_run(U0_FFN2 + 4, U0_PLEW)
                    straight(U0_PLEW, U0_PLEW + 2)
                    pool_residual(pool, N_F2POST)
                    straight(U0_PLEG, U0_PLEG + 2)
                    pool_apply(pool, N_PPRE)
                    straight(U0_PLEG + 2, UNITS)
                    pool_residual(pool, N_PPOST)

                @block.tensor
                def _(pe):
                    pe.sem_inc(unit_done, SPLIT)
                    pe_ffn(pe, 0, U0_FFN1)
                    pe_mixer(pe)
                    pe_ffn(pe, 1, U0_FFN2)
                    pe_ple(pe)

                @block.scalar
                def _(act):
                    act.sem_inc(y_ready, 4)
                    act.sem_inc(sig_done, 2)
                    act.preload_act_table_set(ROOT_SET)
                    act_ffn(act, L, 0, U0_FFN1)
                    act_mixer(act, L)
                    act_ffn(act, L, 1, U0_FFN2)
                    act_ple(act)
                    act.wait_ge(outs, 16 * N_OUTS)

                @block.vector
                def _(dve):
                    dve.sem_inc(up_mul, 2)
                    dve.sem_inc(s_ready, 2)
                    ly = bass.ds(L, 1)
                    dve.tensor_copy(gains[:].rearrange("p (n l k) -> p n l k", n=8, l=1), gains_all[:, :, ly, :]).then_inc(par_ready, 1)
                    dve.tensor_copy(taps[:].rearrange("p w c -> p (w c)").unsqueeze(1), taps_all[:, ly, :]).then_inc(par_ready, 1)
                    dve.tensor_copy(crow[:].unsqueeze(2), rows_all[:, 0:6 * DEPTH].rearrange("p (r l c) -> p r l c", r=3, l=DEPTH)[:, :, ly, :]).then_inc(par_ready, 1)
                    dve.tensor_copy(hgn[:], rows_all[:, 6 * DEPTH:7 * DEPTH][:, ly]).then_inc(par_ready, 1)
                    dve.tensor_copy(lb[:].unsqueeze(1), lb_all[:, ly, :]).then_inc(par_ready, 1)
                    for g in range(2):
                        half = slice(64 * g, 64 * g + 64)
                        dve.tensor_copy(sinkcol[half, :].unsqueeze(1), sinks_all[half, ly, :, g]).then_inc(par_ready, 1)
                    dve.wait_ge(par_ready, 7)
                    for k in range(KD):
                        dve_add_square(dve, N_F1PRE, k)
                    dve_ffn(dve, 0, U0_FFN1)
                    dve_residual(dve, N_F1POST, y)
                    dve_mixer(dve, L)
                    dve_ffn(dve, 1, U0_FFN2)
                    dve_ple(dve)

            with nc.Block() as block:

                @block.vector
                def _(dve):
                    for x in per_layer:
                        dve.sem_clear(x)

        with nc.Block() as block:

            @block.tensor
            def _(pe):
                for t in range(TB):
                    n = tok_n(t)
                    if t >= 4:
                        pe.wait_ge(placed, n_placed[0] + t - 3)
                    for k in range(KD):
                        ins = pe.transpose(ps[0:n, 2 * (t % 4) + k // 4, 128 * (k % 4):128 * (k % 4) + 128], h[:, k, 128 * t:128 * t + n], ident[:])
                    ins.then_inc(turned, 1)

            @block.vector
            def _(dve):
                for t in range(TB):
                    n = tok_n(t)
                    dve.wait_ge(turned, KD + 2 + t + 1)
                    dve.tensor_copy(xtok[0:n, t, :], ps[0:n, 2 * (t % 4):2 * (t % 4) + 2, :].rearrange("p a n -> p (a n)")).then_inc(placed, 1)

            @block.sync
            def _(sp_):
                for t in range(TB):
                    n = tok_n(t)
                    sp_.wait_ge(placed, n_placed[0] + t + 1)
                    dst = o["y_prompt"][0, 128 * t:128 * t + 128, :] if t < 4 else o["y_sample"][0]
                    sp_.dma_start(dst, xtok[0:n, t, :]).then_inc(out_tok, 16)
                sp_.wait_ge(out_tok, 16 * TB)


OUTS = [
    ("y_prompt", (1, SEQ, D)), ("y_sample", (1, DEC, D)),
    ("conv_prompt", (DEPTH, 1, HIST, 256)), ("conv_sample", (DEPTH, 1, HIST, 256)),
    ("hgrn_prompt", (DEPTH, 1, 4, HD, HD)), ("hgrn_sample", (DEPTH, 1, 4, HD, HD)),
    ("swa_k_prompt", (DEPTH, 1, WINDOW, 2, HD)), ("swa_v_prompt", (DEPTH, 1, WINDOW, 2, HD)),
    ("swa_k_sample", (DEPTH, 1, WINDOW, 2, HD)), ("swa_v_sample", (DEPTH, 1, WINDOW, 2, HD)),
    ("sb_k_prompt", (DEPTH, 1, SEQ, 4, HD)), ("sb_v_prompt", (DEPTH, 1, SEQ, 4, HD)),
    ("sb_k_sample", (DEPTH, 1, DEC, 4, HD)), ("sb_v_sample", (DEPTH, 1, DEC, 4, HD)),
]


def kernel(**inputs):
    import numpy as np
    import concourse.bacc as bacc
    from concourse.bass_utils import run_bass_kernel_spmd

    nc = bacc.Bacc("TRN2", target_bir_lowering=False, num_devices=1)
    arrays, a = {}, {}
    for name, x in inputs.items():
        x = np.ascontiguousarray(x)
        arrays[f"in_{name}"] = x
        a[name] = nc.dram_tensor(f"in_{name}", x.shape, mybir.dt.from_np(x.dtype), kind="ExternalInput").ap()
    o = {name: nc.dram_tensor(f"out_{name}", shape, F32, kind="ExternalOutput").ap() for name, shape in OUTS}
    trunk(nc, a, o)
    r = run_bass_kernel_spmd(nc, [arrays], core_ids=[0])
    return tuple(r.results[0][f"out_{name}"] for name, _ in OUTS)
```
